# Optimizing a Trainium2 kernel written in Bass

```python
import jax
import jax.numpy as jnp
from jax import lax
import numpy as np

D_MODEL = 1024
BATCH = 1
SEQ = 1024
DEPTH = 2

CHUNK = 128
A_HEADS = 4
A_HEAD_DIM = 128
D_A = A_HEADS * A_HEAD_DIM
B_GROUPS = 4
D_B = 512
B_CONV = 3
D_IN_HYB = 2 * D_A + 3 * D_B
D_CAT = D_A + D_B
D_C = D_MODEL
C_CONV = 31
N_EXPERTS = 16
N_GROUPS = 4
EXPERTS_PER_GROUP = N_EXPERTS // N_GROUPS
TOP_K = 2
D_EXPERT = 256
N_EVEN = (DEPTH + 1) // 2
N_ODD = DEPTH // 2
N_MOD = 6
EPS = 1e-6

kernel_name = 'hybrid_sgu_shortconv_conformer_grouped_moe_adaln'

def rms_norm(x, g):
    xf = x.astype(jnp.float32)
    y = xf * lax.rsqrt(jnp.mean(xf * xf, axis=-1, keepdims=True) + EPS)
    return (y * g.astype(jnp.float32)).astype(x.dtype)

def layer_norm(x, g, b):
    xf = x.astype(jnp.float32)
    mu = jnp.mean(xf, axis=-1, keepdims=True)
    var = jnp.mean(jnp.square(xf - mu), axis=-1, keepdims=True)
    y = (xf - mu) * lax.rsqrt(var + EPS)
    return (y * g.astype(jnp.float32) + b.astype(jnp.float32)).astype(x.dtype)

def modulate(h, shift, scale):
    return h * (1.0 + scale[:, None, :]) + shift[:, None, :]

def causal_dw_conv(x, w):
    k = w.shape[0]
    return lax.conv_general_dilated(
        x, w[:, None, :].astype(x.dtype), window_strides=(1,),
        padding=[(k - 1, 0)], dimension_numbers=('NWC', 'WIO', 'NWC'),
        feature_group_count=x.shape[-1])

def chunked_sgu(u, v, ln_g, ln_b, w_s, b_s):
    bsz, s_len, _ = v.shape
    v = layer_norm(v, ln_g, ln_b)
    v = v.reshape(bsz, s_len // CHUNK, CHUNK, A_HEADS, A_HEAD_DIM)
    mask = jnp.tril(jnp.ones((CHUNK, CHUNK), dtype=bool))
    w = jnp.where(mask[None], w_s, jnp.zeros_like(w_s))
    s = jnp.einsum('hts,bnshd->bnthd', w, v) + b_s.T[None, None, :, :, None]
    return u * s.reshape(bsz, s_len, D_A)

def hybrid_ab(h, w_in, ln_g, ln_b, w_s, b_s, conv_w, w_out):
    z = h @ w_in
    u, v, bg, cg, hb = jnp.split(
        z, [D_A, 2 * D_A, 2 * D_A + D_B, 2 * D_A + 2 * D_B], axis=-1)
    y_a = chunked_sgu(jax.nn.gelu(u, approximate=False),
                      jax.nn.gelu(v, approximate=False), ln_g, ln_b, w_s, b_s)
    y_b = bg * causal_dw_conv(cg * hb, conv_w)
    return jnp.concatenate([y_a, y_b], axis=-1) @ w_out

def conformer_conv(h, w1, b1, dw_w, dw_b, ln_g, ln_b, w2, b2):
    z = jax.nn.glu(h @ w1 + b1, axis=-1)
    z = causal_dw_conv(z, dw_w) + dw_b
    z = jax.nn.silu(layer_norm(z, ln_g, ln_b))
    return z @ w2 + b2

def grouped_moe(h, router_w, router_bias, w_gate, w_up, w_down):
    bsz, s_len, d = h.shape
    t = h.reshape(-1, d)
    scores = jax.nn.sigmoid(t.astype(jnp.float32) @ router_w.astype(jnp.float32))
    biased = scores + router_bias.astype(jnp.float32)
    grp = biased.reshape(-1, N_GROUPS, EXPERTS_PER_GROUP)
    grp_score = jnp.sum(lax.top_k(grp, TOP_K)[0], axis=-1)
    best = jnp.argmax(grp_score, axis=-1)
    in_group = (jnp.arange(N_EXPERTS) // EXPERTS_PER_GROUP)[None, :] == best[:, None]
    masked = jnp.where(in_group, biased, -jnp.inf)
    _, idx = lax.top_k(masked, TOP_K)
    wsel = jnp.take_along_axis(scores, idx, axis=-1)
    wsel = wsel / jnp.sum(wsel, axis=-1, keepdims=True)
    gates = jnp.sum(jax.nn.one_hot(idx, N_EXPERTS, dtype=jnp.float32) * wsel[..., None],
                    axis=1).astype(h.dtype)
    a = jax.nn.silu(jnp.einsum('td,edf->tef', t, w_gate)) * jnp.einsum('td,edf->tef', t, w_up)
    y = jnp.einsum('tef,efd->td', a * gates[:, :, None], w_down)
    return y.reshape(bsz, s_len, d)

def setup_inputs(seed: int = 0) -> dict:
    key = jax.random.key(seed)
    ks = jax.random.split(key, 32)
    f32 = jnp.float32

    def nrm(k, shape, scale):
        return jax.random.normal(k, shape, f32) * scale

    d = D_MODEL
    return {
        'x': nrm(ks[0], (BATCH, SEQ, d), 1.0),
        'c': nrm(ks[1], (BATCH, d), 1.0),
        'ada_w': nrm(ks[2], (DEPTH, d, N_MOD * d), 0.5 * d ** -0.5),
        'ada_b': nrm(ks[3], (DEPTH, N_MOD * d), 0.02),
        'norm_mix_g': 1.0 + nrm(ks[4], (DEPTH, d), 0.02),
        'norm_ffn_g': 1.0 + nrm(ks[5], (DEPTH, d), 0.02),
        'hyb_w_in': nrm(ks[6], (N_EVEN, d, D_IN_HYB), d ** -0.5),
        'sgu_ln_g': 1.0 + nrm(ks[7], (N_EVEN, D_A), 0.02),
        'sgu_ln_b': nrm(ks[8], (N_EVEN, D_A), 0.02),
        'sgu_w': nrm(ks[9], (N_EVEN, A_HEADS, CHUNK, CHUNK), CHUNK ** -0.5),
        'sgu_b': 1.0 + nrm(ks[10], (N_EVEN, A_HEADS, CHUNK), 0.02),
        'sconv_w': nrm(ks[11], (N_EVEN, B_CONV, D_B), B_CONV ** -0.5),
        'hyb_w_out': nrm(ks[12], (N_EVEN, D_CAT, d), D_CAT ** -0.5),
        'conf_w1': nrm(ks[13], (N_ODD, d, 2 * D_C), d ** -0.5),
        'conf_b1': nrm(ks[14], (N_ODD, 2 * D_C), 0.02),
        'conf_dw_w': nrm(ks[15], (N_ODD, C_CONV, D_C), C_CONV ** -0.5),
        'conf_dw_b': nrm(ks[16], (N_ODD, D_C), 0.02),
        'conf_ln_g': 1.0 + nrm(ks[17], (N_ODD, D_C), 0.02),
        'conf_ln_b': nrm(ks[18], (N_ODD, D_C), 0.02),
        'conf_w2': nrm(ks[19], (N_ODD, D_C, d), D_C ** -0.5),
        'conf_b2': nrm(ks[20], (N_ODD, d), 0.02),
        'router_w': nrm(ks[21], (d, N_EXPERTS), d ** -0.5),
        'router_bias': nrm(ks[22], (N_EXPERTS,), 0.01),
        'moe_w_gate': nrm(ks[23], (DEPTH, N_EXPERTS, d, D_EXPERT), d ** -0.5),
        'moe_w_up': nrm(ks[24], (DEPTH, N_EXPERTS, d, D_EXPERT), d ** -0.5),
        'moe_w_down': nrm(ks[25], (DEPTH, N_EXPERTS, D_EXPERT, d), D_EXPERT ** -0.5),
        'final_norm_g': 1.0 + nrm(ks[26], (d,), 0.02),
    }

def reference(x, c, ada_w, ada_b, norm_mix_g, norm_ffn_g, hyb_w_in, sgu_ln_g, sgu_ln_b,
              sgu_w, sgu_b, sconv_w, hyb_w_out, conf_w1, conf_b1, conf_dw_w, conf_dw_b,
              conf_ln_g, conf_ln_b, conf_w2, conf_b2, router_w, router_bias, moe_w_gate,
              moe_w_up, moe_w_down, final_norm_g):
    c_act = jax.nn.silu(c)
    for l in range(DEPTH):
        mod = c_act @ ada_w[l] + ada_b[l]
        sh1, sc1, g1, sh2, sc2, g2 = jnp.split(mod, N_MOD, axis=-1)
        h = modulate(rms_norm(x, norm_mix_g[l]), sh1, sc1)
        i = l // 2
        if l % 2 == 0:
            y = hybrid_ab(h, hyb_w_in[i], sgu_ln_g[i], sgu_ln_b[i], sgu_w[i], sgu_b[i],
                          sconv_w[i], hyb_w_out[i])
        else:
            y = conformer_conv(h, conf_w1[i], conf_b1[i], conf_dw_w[i], conf_dw_b[i],
                               conf_ln_g[i], conf_ln_b[i], conf_w2[i], conf_b2[i])
        x = x + g1[:, None, :] * y
        h = modulate(rms_norm(x, norm_ffn_g[l]), sh2, sc2)
        x = x + g2[:, None, :] * grouped_moe(h, router_w, router_bias, moe_w_gate[l],
                                             moe_w_up[l], moe_w_down[l])
    return rms_norm(x, final_norm_g)


_drawn_inputs = setup_inputs


def setup_inputs(seed=0):
    import zlib

    import numpy as np

    out = dict(_drawn_inputs(seed))
    spreads = {}
    factors = {'sgu_ln_g': 47.125,
     'sgu_ln_b': 42.377,
     'sgu_b': 24.185,
     'conf_b1': 7.77,
     'conf_dw_b': 3.899,
     'conf_ln_g': 48.745,
     'conf_ln_b': 46.202,
     'conf_b2': 33.6,
     'final_norm_g': 21.245,
     'norm_ffn_g': 3.395}
    for name, (base, spread) in spreads.items():
        noise = np.random.default_rng([zlib.crc32(name.encode()), seed]).standard_normal(out[name].shape)
        drawn = base * np.exp(spread * noise) if base else spread * noise
        out[name] = jnp.asarray(drawn.astype(out[name].dtype))
    for name, factor in factors.items():
        out[name] = (out[name] * factor).astype(out[name].dtype)
    return out
```

```python
from contextlib import ExitStack

import numpy as np

import concourse.bass as bass
from concourse import mybir

F32 = mybir.dt.float32
I32 = mybir.dt.int32
U32 = mybir.dt.uint32
ALU = mybir.AluOpType
ACT = mybir.ActivationFunctionType
AX = mybir.AxisListType

P = 128
D = 1024
T = 1024
KC = D // P
NB = T // P
NL = 2
HT = 512
NH = 2
DA = 512
HEADS = 4
NE = 16
NG = 4
EG = NE // NG
FE = 256
TOPK = 2
CTAPS = 31
BTAPS = 3
LEAST = T * TOPK // P
MOST = LEAST + NE - 1
MAXT = MOST + 1
EPS = 1e-6
BIG = 1e30

COL_ADAB, COL_NMIX, COL_NFFN = 0, 96, 112
COL_SC, COL_B1, COL_DWB, COL_LNG, COL_LNB, COL_C = 128, 140, 156, 164, 172, 180
COL_DW = 188
NTAB_B = 60
NDW = CTAPS * KC
NPT = COL_DW + NDW

QW = 256
NADA = NL * 6 * D // QW
NADA0 = 2 * D // QW
WV, WCG, WHB, WBG, WU, WWO, NW0 = 0, 2, 4, 6, 8, 10, 14
BESIDE = []
_n = NADA0
for _w in range(NW0):
    _k = -(-(NADA - _n) // (NW0 - _w))
    BESIDE.append(list(range(_n, _n + _k)))
    _n += _k
ITEMS = [("a", n) for n in range(NADA0)]
for _w in range(NW0):
    ITEMS += [("w", _w)] + [("a", n) for n in BESIDE[_w]]
NSLOT = 8
SLOT = KC * QW
EXP = KC * 2 * FE + 2 * D
NEB = 3
ITEM0 = len(ITEMS)
NW1 = 12

GROUPS = {}
CONSUMER = []
for _name, _who in (("v", "A" * 8), ("cg", "A" * 8), ("sgu", "D" * 8), ("hb", "D" * 8),
                    ("bg", "D" * 8), ("u", "A" * 8), ("wo", "D" * 16), ("w1", "AD" * 16),
                    ("mu", "D" * 2), ("var", "A" * 2), ("w2", "D" * 16)):
    GROUPS[_name] = len(CONSUMER)
    CONSUMER += list(_who)


USED0 = [GROUPS[_g] + 4 * (_j + 1) for _g, _m in (("v", 2), ("cg", 2), ("hb", 2), ("bg", 2), ("u", 2),
                                                  ("wo", 4)) for _j in range(_m)]
USED1 = ([GROUPS["w1"] + 8 * (_j // 2 + 1) for _j in range(8)]
         + [GROUPS["w2"] + 4 * (_j + 1) for _j in range(4)])


def emptied(g):
    return CONSUMER[:g + 1].count(CONSUMER[g])


def trunk(nc, i, out):
    with ExitStack() as ctx:
        def sb(name, shape, dt=F32):
            return ctx.enter_context(nc.sbuf_tensor(name, shape, dt))

        def sem(name):
            return ctx.enter_context(nc.semaphore(name))

        X = sb("X", [P, NB, D])
        HTR = sb("HTR", [P, KC, T])
        R = sb("R", [P, 4, NB * DA])
        W = sb("W", [P, NEB * EXP])
        PT = sb("PT", [P, NPT])
        MC = sb("MC", [P, NL, 4, KC])
        IDENT = sb("IDENT", [P, P])
        ONES = sb("ONES", [P, P])
        TRI = sb("TRI", [P, P])
        IOTA = sb("IOTA", [P, P])
        RW = sb("RW", [P, KC, NE])
        RB = sb("RB", [P, NE])
        CA = sb("CA", [P, KC])
        EPSC = sb("EPSC", [P, 1])
        SS = sb("SS", [P, NB])
        SD = sb("SD", [P, NB])
        RSTD = sb("RSTD", [P, NB])
        GATE = sb("GATE", [P, TOPK, NB])
        SLOTF = sb("SLOTF", [P, TOPK, NB])
        SLOTU = sb("SLOTU", [P, TOPK, NB], U32)
        TOKI = sb("TOKI", [P, MAXT], U32)
        TCUR = sb("TCUR", [P, 1], U32)
        RT = sb("RT", [1, 5 * MAXT], I32)
        RTF = sb("RTF", [1, 5 * MAXT])
        PSCR = sb("PSCR", [1, 3])
        WT = sb("WT", [P, 8])

        def slot(n):
            return W[:, (n % NSLOT) * SLOT:(n % NSLOT + 1) * SLOT].rearrange("p (k n) -> p k n", k=KC)
        slack = NSLOT * SLOT
        ACC = [W[:, slack + b * QW:slack + (b + 1) * QW] for b in range(2)]
        BROW = [W[0:1, slack + (2 + b) * QW:slack + (3 + b) * QW] for b in range(2)]
        SIG = [W[:, slack + (1 + b) * HT:slack + (2 + b) * HT] for b in range(2)]

        ZERO = W[:, slack + 2 * HT:slack + 4 * HT]

        def r3(n, a):
            return R[:, n, :].rearrange("p (a b) -> p a b", a=a)
        XN = [r3(0, 4), r3(2, 4)]
        V = r3(0, NB)
        PB = r3(1, 4)
        YC = R[:, 2:4, :].rearrange("p r (c t) -> p (r c) t", t=T)
        TABS = R[:, 1, 0:4 * P].rearrange("p (a b) -> p a b", a=4)
        SGW = R[:, 3, 0:HT].rearrange("p (a b) -> p a b", a=HEADS)
        SGT = R[:, 3, HT:2 * HT].rearrange("p (a b) -> p a b", a=HEADS)
        LNG = R[:, 3, 2 * HT:3 * HT]
        LNB = R[:, 3, 3 * HT:4 * HT]
        SBB = R[:, 3, 4 * HT:5 * HT].rearrange("p (a b) -> p a b", a=HEADS)
        BST = R[:, 3, 5 * HT:5 * HT + 6 * NB].rearrange("p (a b) -> p a b", b=6)
        MV = R[:, 3, 5 * HT + 64:5 * HT + 64 + 2 * NB].rearrange("p (a b) -> p a b", b=2)
        GU = [R[:, 0, b * HT:(b + 1) * HT] for b in range(2)]
        GB0 = R[:, 0, 2 * HT:4 * HT]
        TMPO = [R[:, 1, b * HT:(b + 1) * HT] for b in range(2)]
        GT = R[:, 0:2, :].rearrange("p r (c t) -> p (r c) t", t=T)
        CV = YC
        MUB = [R[:, 0, b * HT:(b + 1) * HT] for b in range(2)]
        SQ = [R[:, 0, (2 + b) * HT:(3 + b) * HT] for b in range(2)]
        RSB = [R[:, 0, (4 + b) * HT:(5 + b) * HT] for b in range(2)]
        GB1 = R[:, 1, 0:D]
        B2B = R[:, 1, D:2 * D]
        TMP1 = [R[:, 1, 2 * D + b * HT:2 * D + (b + 1) * HT] for b in range(2)]
        XG = R[:, 1, 0:D]
        XT = R[:, 1, D:2 * D].rearrange("p (k t) -> p k t", k=KC)
        YS = R[:, 1, 2 * D:3 * D]
        SG = R[:, 1, 3 * D:3 * D + FE]
        AG = R[:, 1, 3 * D + FE:3 * D + 2 * FE]
        AT = R[:, 1, 3 * D + 2 * FE:3 * D + 3 * FE].rearrange("p (k t) -> p k t", k=2)
        JUNK = R[:, 1, 3 * D:4 * D]
        ne = NB * NE

        def rt(n, a=NB):
            return R[:, 3, n * ne:(n + 1) * ne].rearrange("p (a b) -> p a b", a=a)
        SCO, BIA, MSK, OH1, OH2, MM, TA, TB, PRI = (rt(n) for n in range(9))
        SM = R[:, 3, 9 * ne:10 * ne]
        QO = R[:, 3, 10 * ne:14 * ne].rearrange("p (a b) -> p a b", b=MAXT)
        RO = R[:, 3, 14 * ne:30 * ne].rearrange("p (a b) -> p a b", b=P)
        ROWT = R[0:1, 3, 30 * ne:30 * ne + 2 * P]
        TOKF = WT
        def hv(n):
            return HTR[:, n, :]
        Y1 = [hv(0), hv(1)]
        Y2 = [hv(2), hv(3)]
        YM = [hv(4), hv(5)]
        GBF = hv(6)
        FGB = hv(7)
        OUTS = [hv(0), hv(1), hv(2), hv(3)]

        bank = [ctx.enter_context(nc.psum_tensor(f"bank{n}", [P, HT], F32)) for n in range(8)]
        M = bank[0:4]
        TB_ = bank[4:6]
        X0, X1 = bank[6], bank[7]

        xn_dram = nc.dram_tensor("xn_scratch", (T, D), F32, kind="Internal").ap()
        y_dram = nc.dram_tensor("y_scratch", (MOST * P, D), F32, kind="Internal").ap()
        g_dram = nc.dram_tensor("gate_scratch", (4, D), F32, kind="Internal").ap()

        xl = [sem(f"x_loaded{n}") for n in range(2)]
        tabs_in = sem("table_rows_loaded")
        small_in = sem("small_params_loaded")
        sgu_in = sem("sgu_params_loaded")
        const = sem("constants_made")
        pt_ps = sem("param_transpose_done")
        pt_ok = sem("param_columns_ready")
        ca_ok = sem("c_act_ready")
        sgw_ok = sem("sgu_w_masked")
        sgt_ps = sem("sgu_w_transposed")
        sgt_ok = sem("sgu_w_columns_ready")
        ring = [sem(f"ring_slot_loaded{n}") for n in range(NSLOT)]
        ada_used = sem("ada_group_summed")
        red = sem("ada_reduced")
        ada_fin = sem("ada_finished")
        brow_in = [sem(f"gate_bias_row_loaded{n}") for n in range(2)]
        brow_out = [sem(f"gate_row_stored{n}") for n in range(2)]
        zeroed = sem("scratch_rows_zeroed")
        rms_sd = sem("rms_root_ready")
        xn_ok = sem("xn_ready")
        xn_out = [sem(f"xn_stored{n}") for n in range(2)]
        tr = sem("xn_transposed")
        tev_a = sem("ht_evicted_by_act")
        tev_d = sem("ht_evicted_by_dve")
        full = sem("main_bank_full")
        free = {"A": sem("main_bank_emptied_by_act"), "D": sem("main_bank_emptied_by_dve")}
        ln_var = sem("ln_variance_ready")
        ln_sd = sem("ln_root_ready")
        v_ok = sem("v_normed")
        s_ok = sem("spatial_gate_ready")
        p_ok = sem("conv_product_ready")
        u_ok = sem("gelu_u_ready")
        ya_ok = sem("head_a_output_ready")
        gb_in = [sem(f"gate_rows_in{n}") for n in range(4)]
        xup = sem("x_updated")
        dch = sem("dve_step")
        act_ch = sem("act_step")
        sig_ok = sem("sigmoid_ready")
        conv_ok = sem("conv_ready")
        cen_ok = sem("centred")
        sq1_ok = sem("squares_ready")
        sq1_used = sem("squares_used")
        nrm_ok = sem("normalised")
        z_ok = sem("z_ready")
        lg = sem("logits_done")
        sco_ok = sem("scores_ready")
        mm_ok = sem("choice_mask_ready")
        cnt = sem("counts_done")
        oh_ok = sem("slot_one_hots_ready")
        tok_ps = sem("slot_tokens_done")
        tab_ok = sem("tables_ready")
        e_in = [[sem(f"expert_loaded{l}_{b}") for b in range(NEB)] for l in range(NL)]
        xg_in = [sem(f"tile_gathered{l}") for l in range(NL)]
        cur_ok = [sem(f"tile_tokens_copied{l}") for l in range(NL)]
        held = [sem(f"gather_waits_met{l}") for l in range(NL)]
        xtr = [sem(f"tile_transposed{l}") for l in range(NL)]
        xt_a = [sem(f"tile_evicted_by_act{l}") for l in range(NL)]
        xt_d = [sem(f"tile_evicted_by_dve{l}") for l in range(NL)]
        gu = [sem(f"gate_up_done{l}") for l in range(NL)]
        sg_ok = [sem(f"silu_ready{l}") for l in range(NL)]
        ag_ok = [sem(f"hidden_ready{l}") for l in range(NL)]
        atr = [sem(f"hidden_transposed{l}") for l in range(NL)]
        at_ok = [sem(f"hidden_columns_ready{l}") for l in range(NL)]
        dn = [sem(f"down_done{l}") for l in range(NL)]
        ys_a = [sem(f"tile_out_by_act{l}") for l in range(NL)]
        ys_d = [sem(f"tile_out_by_dve{l}") for l in range(NL)]
        y_out = [sem(f"tile_stored{l}") for l in range(NL)]
        c_in = [[[sem(f"combine_in{l}_{b}_{s}") for s in range(2)] for b in range(2)] for l in range(NL)]
        ym_ok = sem("first_choice_scaled")
        out_ok = sem("output_block_ready")
        o_out = [sem(f"output_stored{n}") for n in range(4)]

        def cols(w, c0):
            return w.rearrange("(k p) n -> p k n", p=P)[:, :, c0:c0 + QW]
        w_in, w_out = i["hyb_w_in"][0], i["hyb_w_out"][0]
        W0 = [cols(w_in, sec * DA + h * QW) for sec in (1, 3, 4, 2, 0) for h in range(2)]
        W0 += [cols(w_out, h * QW) for h in range(4)]
        w1, w2 = i["conf_w1"][0], i["conf_w2"][0]
        W1 = [cols(w1, part * D + h * QW) for h in range(4) for part in (1, 0)]
        W1 += [cols(w2, h * QW) for h in range(4)]
        x_rows = i["x"][0].rearrange("(b p) d -> p b d", p=P)
        out_rows = out[0].rearrange("(b p) d -> p b d", p=P)
        rows = {n: i[n].rearrange("a (r q) -> (a r) q", q=P)
                for n in ("ada_b", "norm_mix_g", "norm_ffn_g", "conf_b1", "conf_dw_b", "conf_ln_g",
                          "conf_ln_b", "c")}
        rows["sconv"] = i["sconv_w"][0].rearrange("j (r q) -> (j r) q", q=P)
        rows["dw"] = i["conf_dw_w"][0].rearrange("j (r q) -> (j r) q", q=P)

        def on_all(v, n):
            return v.rearrange("(a n) -> a n", a=1).broadcast_to([P, n])

        def item_at(kind, n):
            return ITEMS.index((kind, n))

        def wait_item(eng, at):
            eng.wait_ge(ring[at % NSLOT], 16 * (at // NSLOT + 1))

        def wait_used(eng, at):
            kind, n = ITEMS[at]
            if kind == "a":
                eng.wait_ge(ada_used, n + 1)
            else:
                eng.wait_ge(full, USED0[n])

        block = ctx.enter_context(nc.Block())

        @block.sync
        def _(sp):
            for at, (kind, n) in enumerate(ITEMS):
                if at >= NSLOT:
                    wait_used(sp, at - NSLOT)
                src = W0[n] if kind == "w" else cols(i["ada_w"][n // 24], (n % 24) * QW)
                sp.dma_start(slot(at), src).then_inc(ring[at % NSLOT], 16)

            def expert(l, e, b):
                g = i["moe_w_gate"][l].rearrange("e (k p) f -> e p k f", p=P)
                u = i["moe_w_up"][l].rearrange("e (k p) f -> e p k f", p=P)
                dw = i["moe_w_down"][l].rearrange("e (k p) n -> e p k n", p=P)
                at = b * EXP
                wgu = W[:, at:at + 2 * KC * FE].rearrange("p (k n) -> p k n", k=KC)
                wd = W[:, at + 2 * KC * FE:at + EXP].rearrange("p (k n) -> p k n", k=2)
                s = e_in[l][b]
                pick = (lambda w: w[bass.ds(e, 1)].rearrange("e p k n -> (e p) k n")) if not isinstance(e, int) else (lambda w: w[e])
                sp.dma_start(wgu[:, :, 0:FE], pick(g)).then_inc(s, 16)
                sp.dma_start(wgu[:, :, FE:2 * FE], pick(u)).then_inc(s, 16)
                sp.dma_start(wd, pick(dw)).then_inc(s, 16)

            def experts(l):
                for e in range(NEB):
                    expert(l, e, e)
                sp.wait_ge(tab_ok, l + 1)

                def after(e3):
                    done = sp.value_load(RT[0:1, bass.ds(e3 + 1, 1)], min_val=1, max_val=MAXT)
                    sp.wait_ge(dn[l], done)
                with sp.Fori(1, NE // NEB) as j:
                    for b in range(NEB):
                        after(j * NEB + (b - NEB))
                        expert(l, j * NEB + b, b)
                last = NE - 1
                after(last - NEB)
                expert(l, last, last % NEB)
                return sp.value_load(RT[0:1, 0:1], min_val=1, max_val=MOST)

            sp.wait_ge(full, USED0[-1])
            sp.wait_ge(ada_fin, NADA)
            sp.wait_ge(brow_out[0], 16 * 8)
            sp.wait_ge(brow_out[1], 16 * 8)
            sp.wait_ge(zeroed, 16)
            nt = experts(0)
            sp.wait_ge(dn[0], nt)
            for n in range(NW1):
                if n >= NSLOT:
                    sp.wait_ge(full, USED1[n - NSLOT])
                sp.dma_start(slot(n), W1[n]).then_inc(ring[n % NSLOT], 16)
            sp.wait_ge(full, USED1[-1])
            sp.wait_ge(free["D"], emptied(GROUPS["mu"] - 1))
            experts(1)
            for b in range(NB):
                sp.wait_ge(out_ok, b + 1)
                sp.dma_start(out_rows[:, b, :], OUTS[b % 4]).then_inc(o_out[b % 4], 16)
            for n in range(4):
                sp.wait_ge(o_out[n], 16 * (NB // 4))

        @block.gpsimd
        def _(pool):
            pool.dma_start(TABS[0:96, 0, :], rows["ada_b"]).then_inc(tabs_in, 16)
            pool.dma_start(TABS[96:112, 0, :], rows["norm_mix_g"]).then_inc(tabs_in, 16)
            pool.dma_start(TABS[112:128, 0, :], rows["norm_ffn_g"]).then_inc(tabs_in, 16)
            at = 0
            for name, n in (("sconv", 12), ("conf_b1", 16), ("conf_dw_b", 8), ("conf_ln_g", 8),
                            ("conf_ln_b", 8), ("c", 8)):
                pool.dma_start(TABS[at:at + n, 1, :], rows[name]).then_inc(tabs_in, 16)
                at += n
            pool.dma_start(TABS[:, 2, :], rows["dw"][0:P]).then_inc(tabs_in, 16)
            pool.dma_start(TABS[0:NDW - P, 3, :], rows["dw"][P:NDW]).then_inc(tabs_in, 16)
            pool.memset(IDENT[:], 0.0).then_inc(const, 1)
            pool.memset(ONES[:], 1.0).then_inc(const, 1)
            pool.memset(EPSC[:], EPS).then_inc(const, 1)
            pool.wait_ge(const, 3)
            pool.affine_select(out=IDENT[:], in_=IDENT[:], compare_op=ALU.not_equal, fill=1.0,
                               base=0, pattern=[[-1, P]], channel_multiplier=1).then_inc(const, 1)
            pool.affine_select(out=TRI[:], in_=ONES[:], compare_op=ALU.is_gt, fill=0.0,
                               base=0, pattern=[[1, P]], channel_multiplier=-1).then_inc(const, 1)
            pool.iota(IOTA[:], pattern=[[1, P]], base=0, channel_multiplier=0,
                      allow_small_or_imprecise_dtypes=True).then_inc(const, 1)
            pool.iota(TOKF[:], pattern=[[P, NB]], base=0, channel_multiplier=1,
                      allow_small_or_imprecise_dtypes=True).then_inc(const, 1)
            pool.memset(PSCR[:], 0.0).then_inc(const, 1)
            pool.memset(ZERO, 0.0).then_inc(const, 1)
            pool.wait_ge(sgu_in, 64)
            pool.affine_select(out=SGW, in_=SGW, compare_op=ALU.is_ge, fill=0.0, base=0,
                               pattern=[[0, HEADS], [-1, P]], channel_multiplier=1).then_inc(sgw_ok, 1)

            pool.wait_ge(const, 9)
            rest = y_dram[LEAST * P:MOST * P, :].rearrange("(t p) d -> p t d", p=P)
            pool.dma_start(rest, ZERO.unsqueeze(1).broadcast_to([P, MOST - LEAST, D])).then_inc(zeroed, 16)
            for q in range(16):
                l, s = q // 8, (2, 5)[q // 4 % 2]
                n = 24 * l + 4 * s + q % 4
                if q >= 2:
                    pool.wait_ge(brow_out[q % 2], 16 * (q // 2))
                pool.dma_start(BROW[q % 2], i["ada_b"][l:l + 1, s * D + q % 4 * QW:s * D + (q % 4 + 1) * QW]
                               ).then_inc(brow_in[q % 2], 16)
                pool.wait_ge(ada_fin, n + 1)
                pool.dma_start(g_dram[q // 4:q // 4 + 1, q % 4 * QW:(q % 4 + 1) * QW], BROW[q % 2]
                               ).then_inc(brow_out[q % 2], 16)

            for l in range(NL):
                for b in range(NB):
                    pool.wait_ge(xn_ok, 8 * (2 * l + 1) + b + 1)
                    pool.dma_start(xn_dram[P * b:P * b + P, :], XN[b // 4][:, b % 4, :]).then_inc(xn_out[l], 16)
                pool.wait_ge(tab_ok, l + 1)
                pool.wait_ge(xn_out[l], 16 * NB)
                nt = pool.value_load(RT[0:1, 0:1], min_val=1, max_val=MOST)

                def gather():
                    return pool.indirect_dma_start(
                        out=XG, out_offset=None, in_=xn_dram,
                        in_offset=bass.IndirectOffsetOnAxis(ap=TCUR[:, 0:1], axis=0)).then_inc(xg_in[l], 16)
                pool.tensor_tensor(PSCR[:, l:l + 1], PSCR[:, 2:3], PSCR[:, 2:3], ALU.add).then_inc(held[l], 1)
                pool.tensor_copy(TCUR[:], TOKI[:, 0:1]).then_inc(cur_ok[l], 1)
                pool.wait_ge(cur_ok[l], 1)
                gather()
                with pool.Fori(0, nt) as t:
                    pool.wait_ge(xg_in[l], t * 16 + 16)
                    pool.tensor_copy(TCUR[:], TOKI[:, bass.ds(t + 1, 1)]).then_inc(cur_ok[l], 1)
                    pool.wait_ge(cur_ok[l], t + 2)
                    pool.wait_ge(xtr[l], t + 1)
                    pool.wait_ge(held[l], t + 1)
                    pool.tensor_tensor(PSCR[:, l:l + 1], PSCR[:, 2:3], PSCR[:, 2:3], ALU.add).then_inc(held[l], 1)
                    gather()
                pool.wait_ge(zeroed, 16)
                pool.wait_ge(y_out[l], nt * 16 + 16)
                pool.wait_ge(xg_in[l], nt * 16 + 16)
                pool.wait_ge(held[l], nt + 1)
                pool.tensor_tensor(PSCR[:, l:l + 1], PSCR[:, 2:3], PSCR[:, 2:3], ALU.add).then_inc(held[l], 1)
                for b in range(NB):
                    if b >= 2:
                        pool.wait_ge(ym_ok, l * NB + b - 1)
                        pool.wait_ge(xup, 16 * l + 8 + b - 1)
                    for s, dst in ((0, Y1), (1, Y2)):
                        pool.indirect_dma_start(
                            out=dst[b % 2], out_offset=None, in_=y_dram,
                            in_offset=bass.IndirectOffsetOnAxis(ap=SLOTU[:, s, b:b + 1], axis=0)
                        ).then_inc(c_in[l][b % 2][s], 16)

        @block.scalar
        def _(act):
            for n in range(2):
                act.dma_start(X[:, 4 * n:4 * n + 4, :], x_rows[:, 4 * n:4 * n + 4, :]).then_inc(xl[n], 16)
            act.dma_start(SGW, i["sgu_w"][0].rearrange("h t s -> t h s")).then_inc(sgu_in, 16)
            act.dma_start(LNG, on_all(i["sgu_ln_g"][0], DA)).then_inc(sgu_in, 16)
            act.dma_start(LNB, on_all(i["sgu_ln_b"][0], DA)).then_inc(sgu_in, 16)
            act.dma_start(SBB.rearrange("p a b -> p (a b)"),
                          on_all(i["sgu_b"][0].rearrange("h t -> (h t)"), HEADS * P)).then_inc(sgu_in, 16)
            act.dma_start(RW[:], i["router_w"].rearrange("(k p) e -> p k e", p=P)).then_inc(small_in, 16)
            act.dma_start(RB[:], on_all(i["router_bias"], NE)).then_inc(small_in, 16)
            act.wait_ge(pt_ok, 2)
            act.activation(CA[:], PT[:, COL_C:COL_C + KC], ACT.Silu).then_inc(ca_ok, 1)

            steps = [0]

            def link(ins):
                steps[0] += 1
                ins.then_inc(act_ch, 1)
                act.wait_ge(act_ch, steps[0])

            def gate_rows(dst, n):
                for b in range(2):
                    act.wait_ge(brow_out[b], 32 * (n + 1))
                act.dma_start(dst, on_all(g_dram[n], D)).then_inc(gb_in[n], 16)

            def rms_sums(r):
                for h in range(NH):
                    if r == 0:
                        act.wait_ge(xl[h], 16)
                    for b in range(4 * h, 4 * h + 4):
                        if r:
                            act.wait_ge(xup, 8 * (r - 1) + b + 1)
                        link(act.activation(JUNK, X[:, b, :], ACT.Square, accum_out=SS[:, b:b + 1]))
                    s = slice(4 * h, 4 * h + 4)
                    act.activation(SD[:, s], SS[:, s], ACT.Sqrt, bias=EPSC[:], scale=1.0 / D).then_inc(rms_sd, 1)

            def evict_ht(r, l, ffn):
                for h in range(NH):
                    for k in range(0, KC, 2):
                        act.wait_ge(tr, 16 * r + 8 * h + k + 1)
                        act.wait_ge(ada_fin, NADA0 if r == 0 else NADA)
                        act.activation(HTR[:, k, HT * h:HT * h + HT], TB_[0][:], ACT.Identity,
                                       bias=MC[:, l, 2 * ffn + 1, k:k + 1],
                                       scale=MC[:, l, 2 * ffn, k:k + 1]).then_inc(tev_a, 1)

            def take(g):
                act.wait_ge(full, g + 1)
                return M[g % 4]

            def experts(l):
                act.wait_ge(tab_ok, l + 1)
                nt = act.value_load(RT[0:1, 0:1], min_val=1, max_val=MOST)

                def evict_tile(n_tr):
                    act.wait_ge(xtr[l], n_tr)
                    for k in range(4):
                        ins = act.activation(XT[:, k, :], TB_[0][:, k * P:(k + 1) * P], ACT.Identity,
                                             bias=MC[:, l, 3, k:k + 1], scale=MC[:, l, 2, k:k + 1])
                    ins.then_inc(xt_a[l], 1)
                evict_tile(1)
                act.sem_inc(ys_a[l], 1)
                act.sem_inc(y_out[l], 16)
                with act.Fori(0, nt) as t:
                    act.wait_ge(gu[l], t + 1)
                    act.activation(SG, M[0][:, 0:FE], ACT.Silu).then_inc(sg_ok[l], 1)
                    evict_tile(t + 2)
                    act.wait_ge(dn[l], t + 1)
                    act.wait_ge(y_out[l], t * 16 + 16)
                    act.activation(YS[:, 0:HT], M[1][:], ACT.Copy).then_inc(ys_a[l], 1)
                    act.wait_ge(ys_a[l], t + 2)
                    act.wait_ge(ys_d[l], t + 2)
                    act.dma_start(y_dram[bass.ds(t * P, P), :], YS).then_inc(y_out[l], 16)
                gate_rows(GBF, 2 * l + 1)
                if l == NL - 1:
                    act.dma_start(FGB, on_all(i["final_norm_g"], D)).then_inc(small_in, 16)
                for b in range(NB):
                    act.wait_ge(c_in[l][b % 2][0], 16 * (b // 2 + 1))
                    if b >= 2:
                        act.wait_ge(xup, 16 * l + 8 + b - 1)
                    act.activation(YM[b % 2], Y1[b % 2], ACT.Copy,
                                   scale=GATE[:, 0, b:b + 1]).then_inc(ym_ok, 1)

            def scores(l):
                act.wait_ge(lg, l + 1)
                act.activation(SCO.rearrange("p a b -> p (a b)"), X0[:, 0:ne], ACT.Sigmoid).then_inc(sco_ok, 1)

            rms_sums(0)
            evict_ht(0, 0, 0)
            for n in range(8):
                c, b = QW * (n // 4), 2 * (n % 4)
                act.activation(V[:, b:b + 2, c:c + QW],
                               take(GROUPS["v"] + n)[:].rearrange("p (b c) -> p b c", b=2),
                               ACT.Gelu).then_inc(free["A"], 1)
            act.wait_ge(ln_var, 1)
            act.activation(SD[:], MV[:, :, 1], ACT.Sqrt, bias=EPSC[:]).then_inc(ln_sd, 1)
            for n in range(8):
                act.activation(PB[:, n // 2, HT * (n % 2):HT * (n % 2) + HT],
                               take(GROUPS["cg"] + n)[:], ACT.Copy).then_inc(free["A"], 1)
            act.wait_ge(full, GROUPS["sgu"] + 8)
            gate_rows(GB0, 0)
            for n in range(8):
                if n >= 2:
                    act.wait_ge(ya_ok, n - 1)
                act.activation(GU[n % 2], take(GROUPS["u"] + n)[:], ACT.Gelu).then_inc(free["A"], 1)
            rms_sums(1)
            evict_ht(1, 0, 1)
            scores(0)
            experts(0)
            rms_sums(2)
            evict_ht(2, 1, 0)
            for n in range(16):
                g = GROUPS["w1"] + 2 * n
                if n >= 2:
                    act.wait_ge(free["D"], emptied(g - 3))
                ct = n // 2
                act.activation(SIG[n % 2], take(g)[:], ACT.Sigmoid,
                               bias=PT[:, COL_B1 + KC + ct:COL_B1 + KC + ct + 1]).then_inc(free["A"], 1)
            act.wait_ge(conv_ok, KC)
            gate_rows(GB1, 2)
            act.dma_start(B2B, on_all(i["conf_b2"][0], D)).then_inc(gb_in[2], 16)
            for h in range(NH):
                s = slice(HT * h, HT * h + HT)
                for k in range(KC):
                    act.wait_ge(cen_ok, KC * h + k + 1)
                    m = KC * h + k - 2
                    if m >= 0 and m % KC < KC - 1:
                        act.wait_ge(sq1_used, (KC - 1) * (m // KC) + m % KC + 1)
                    elif m >= 0:
                        act.wait_ge(full, GROUPS["var"] + m // KC + 1)
                    act.activation(SQ[k % 2], CV[:, k, s], ACT.Square).then_inc(sq1_ok, 1)
                act.activation(RSB[h], take(GROUPS["var"] + h)[:], ACT.Sqrt, bias=EPSC[:],
                               scale=1.0 / D).then_inc(free["A"], 1)
            for h in range(NH):
                s = slice(HT * h, HT * h + HT)
                for k in range(KC):
                    act.wait_ge(nrm_ok, KC * h + k + 1)
                    act.activation(CV[:, k, s], CV[:, k, s], ACT.Silu,
                                   bias=PT[:, COL_LNB + k:COL_LNB + k + 1],
                                   scale=PT[:, COL_LNG + k:COL_LNG + k + 1]).then_inc(z_ok, 1)
            rms_sums(3)
            evict_ht(3, 1, 1)
            scores(1)
            experts(1)
            rms_sums(4)

        @block.tensor
        def _(pe):
            pe.wait_ge(const, 7)
            pe.wait_ge(tabs_in, 16 * 11)
            for n, m in enumerate((P, NTAB_B, P, NDW - P)):
                ins = pe.transpose(X0[:, 128 * n:128 * n + m], TABS[0:m, n, :], IDENT[0:m, 0:m])
            ins.then_inc(pt_ps, 1)
            pe.wait_ge(sgw_ok, 1)
            for h in range(HEADS):
                ins = pe.transpose(X1[:, P * h:P * h + P], SGW[:, h, :], IDENT[:])
            ins.then_inc(sgt_ps, 1)

            def reduce_ada(n):
                pe.wait_ge(ada_used, n + 1)
                if n == 0:
                    pe.wait_ge(pt_ok, 4)
                else:
                    pe.wait_ge(ada_fin, n)
                if (n % 24) // 4 in (2, 5):
                    ins = pe.matmul(X0[0:1, 0:QW], ONES[:, 0:1], ACC[n % 2], start=True, stop=True)
                else:
                    for c in range(2):
                        ins = pe.matmul(X0[:, c:c + 1], ACC[n % 2][:, P * c:P * c + P], ONES[:, 0:1],
                                        start=True, stop=True)
                ins.then_inc(red, 1)

            def transposes(r):
                for h in range(NH):
                    for k in range(KC):
                        q = 16 * r + 8 * h + k
                        if k == 0:
                            pe.wait_ge(xn_ok, 8 * r + 4 * h + 4)
                        if q >= 2:
                            pe.wait_ge((tev_a, tev_d)[q % 2], q // 2)
                        for b in range(4):
                            ins = pe.transpose(TB_[q % 2][:, P * b:P * b + P],
                                               XN[h][:, b, P * k:P * k + P], IDENT[:])
                        ins.then_inc(tr, 1)

            def ht_ready(r, h):
                pe.wait_ge(tev_a, 8 * r + 4 * h + 4)
                pe.wait_ge(tev_d, 8 * r + 4 * h + 4)

            def main(g):
                if g >= 4:
                    pe.wait_ge(free[CONSUMER[g - 4]], emptied(g - 4))
                return M[g % 4]

            def product(g, lhs, rhs, kc=KC):
                dst = main(g)
                for k in range(kc):
                    ins = pe.matmul(dst[:], lhs(k), rhs(k), start=(k == 0), stop=(k == kc - 1))
                return ins.then_inc(full, 1)

            def cols_of(g, w, n):
                c, h = n // 2, n % 2
                return product(g, lambda k: w[:, k, P * c:P * c + P],
                               lambda k: HTR[:, k, HT * h:HT * h + HT])

            def rows_of(g, src, w, n):
                dst = main(g)
                for b in range(2):
                    t0 = P * (2 * n + b)
                    for k in range(KC):
                        ins = pe.matmul(dst[:, QW * b:QW * b + QW], src[:, k, t0:t0 + P], w[:, k, :],
                                        start=(k == 0), stop=(k == KC - 1))
                return ins.then_inc(full, 1)

            def item0(wn, g0, of):
                at = item_at("w", wn)
                wait_item(pe, at)
                w = slot(at)
                for n in range(4):
                    of(g0 + n, w, n)
                    if n < len(BESIDE[wn]):
                        reduce_ada(BESIDE[wn][n])

            def experts(l, r):
                for b in range(NB):
                    if b % 4 == 0:
                        ht_ready(r, b // 4)
                    if b == 0:
                        pe.wait_ge(ada_fin, NADA)
                        pe.wait_ge(small_in, 32)
                    for k in range(KC):
                        ins = pe.matmul(X0[:, NE * b:NE * b + NE], HTR[:, k, P * b:P * b + P],
                                        RW[:, k, :], start=(k == 0), stop=(k == KC - 1))
                ins.then_inc(lg, 1)
                pe.wait_ge(mm_ok, l + 1)
                mm = MM.rearrange("p a b -> p (a b)")
                pe.matmul(X1[:, 0:ne], TRI[:], mm, start=True, stop=True)
                pe.matmul(X1[:, ne:2 * ne], ONES[:], mm, start=True, stop=True).then_inc(cnt, 1)
                pe.wait_ge(oh_ok, l + 1)
                for n in range(2 * NB):
                    ins = pe.matmul(X0[:, 0:MAXT], RO[:, n, :], QO[:, n, :], start=(n == 0),
                                    stop=(n == 2 * NB - 1))
                ins.then_inc(tok_ps, 1)
                pe.wait_ge(tab_ok, l + 1)
                nt = pe.value_load(RT[0:1, 0:1], min_val=1, max_val=MOST)
                last = GROUPS["w2"] + 15 if l else GROUPS["wo"] + 15
                pe.wait_ge(free["A"], CONSUMER[:last + 1].count("A"))
                pe.wait_ge(free["D"], CONSUMER[:last + 1].count("D"))

                def transpose_tile(n_in):
                    pe.wait_ge(xg_in[l], n_in)
                    for k in range(KC):
                        ins = pe.transpose(TB_[k // 4][:, P * (k % 4):P * (k % 4) + P],
                                           XG[:, P * k:P * k + P], IDENT[:])
                    ins.then_inc(xtr[l], 1)
                transpose_tile(16)
                with pe.Fori(0, nt) as t:
                    thr = [pe.value_load(RT[0:1, bass.ds(t + MAXT * (1 + b), 1)], min_val=0, max_val=48 * NE)
                           for b in range(NEB)]
                    at = pe.value_load(RT[0:1, bass.ds(t + MAXT * 4, 1)], min_val=0, max_val=(NEB - 1) * EXP)
                    pe.wait_ge(xt_a[l], t + 1)
                    pe.wait_ge(xt_d[l], t + 1)
                    for b in range(NEB):
                        pe.wait_ge(e_in[l][b], thr[b])
                    for k in range(KC):
                        ins = pe.matmul(M[0][:], XT[:, k, :], W[:, bass.ds(at + k * 2 * FE, 2 * FE)],
                                        start=(k == 0), stop=(k == KC - 1))
                    ins.then_inc(gu[l], 1)
                    transpose_tile(t * 16 + 32)
                    pe.wait_ge(ag_ok[l], t + 1)
                    for k in range(2):
                        ins = pe.transpose(X0[:, P * k:P * k + P], AG[:, P * k:P * k + P], IDENT[:])
                    ins.then_inc(atr[l], 1)
                    pe.wait_ge(at_ok[l], t + 1)
                    pe.wait_ge(ys_a[l], t + 1)
                    pe.wait_ge(ys_d[l], t + 1)
                    for h in range(NH):
                        for k in range(2):
                            ins = pe.matmul(M[1 + h][:], AT[:, k, :],
                                            W[:, bass.ds(at + 2 * KC * FE + k * D + h * HT, HT)],
                                            start=(k == 0), stop=(k == 1))
                    ins.then_inc(dn[l], 1)
                pe.wait_ge(ys_a[l], nt + 1)
                pe.wait_ge(ys_d[l], nt + 1)
                pe.wait_ge(xt_a[l], nt + 1)
                pe.wait_ge(xt_d[l], nt + 1)

            for n in range(NADA0):
                reduce_ada(n)
            transposes(0)
            ht_ready(0, 0)
            ht_ready(0, 1)
            for j in range(2):
                item0(WV + j, GROUPS["v"] + 4 * j, lambda g, w, n: rows_of(g, HTR, w, n))
            for j in range(2):
                item0(WCG + j, GROUPS["cg"] + 4 * j, cols_of)
            pe.wait_ge(sgt_ok, 1)
            for n in range(8):
                hd, h = n // 2, n % 2
                dst = main(GROUPS["sgu"] + n)
                for c in range(4):
                    b = 4 * h + c
                    pe.wait_ge(v_ok, b + 1)
                    ins = pe.matmul(dst[:, P * c:P * c + P], V[:, b, P * hd:P * hd + P],
                                    SGT[:, hd, :], start=True, stop=True)
                ins.then_inc(full, 1)
            for name, wn in (("hb", WHB), ("bg", WBG), ("u", WU)):
                for j in range(2):
                    item0(wn + j, GROUPS[name] + 4 * j, cols_of)
            pe.wait_ge(ya_ok, 8)
            pe.wait_ge(free["D"], emptied(GROUPS["bg"] + 7))
            for j in range(4):
                item0(WWO + j, GROUPS["wo"] + 4 * j, lambda g, w, n: rows_of(g, YC, w, n))
            transposes(1)
            experts(0, 1)
            transposes(2)
            def item1(n):
                before = len(range(n % NSLOT, ITEM0, NSLOT))
                pe.wait_ge(ring[n % NSLOT], 16 * (before + n // NSLOT + 1))
                return slot(n)
            ht_ready(2, 0)
            ht_ready(2, 1)
            for j in range(4):
                w = [item1(2 * j), item1(2 * j + 1)]
                for n in range(4):
                    for part in range(2):
                        cols_of(GROUPS["w1"] + 8 * j + 2 * n + part, w[part], n)
            for h in range(NH):
                if h == 0:
                    pe.wait_ge(conv_ok, KC)
                product(GROUPS["mu"] + h, lambda k: ONES[:], lambda k: CV[:, k, HT * h:HT * h + HT])
            for h in range(NH):
                dst = main(GROUPS["var"] + h)
                for k in range(KC):
                    pe.wait_ge(sq1_ok, KC * h + k + 1)
                    ins = pe.matmul(dst[:], ONES[:], SQ[k % 2], start=(k == 0), stop=(k == KC - 1))
                    ins.then_inc(*((sq1_used, 1) if k < KC - 1 else (full, 1)))
            for j in range(4):
                w = item1(8 + j)
                for n in range(4):
                    pe.wait_ge(z_ok, KC * (n // 2) + KC)
                    rows_of(GROUPS["w2"] + 4 * j + n, CV, w, n)
            transposes(3)
            experts(1, 3)

        @block.vector
        def _(dve):
            steps = [0]

            def link(ins):
                steps[0] += 1
                ins.then_inc(dch, 1)
                dve.wait_ge(dch, steps[0])

            def tt(o, a, b, op):
                return dve.tensor_tensor(o, a, b, op)

            for n, m in enumerate((P, NTAB_B, P, NDW - P)):
                dve.wait_ge(pt_ps, 1)
                c0 = (0, P, COL_DW, COL_DW + P)[n]
                dve.tensor_copy(PT[:, c0:c0 + m], X0[:, 128 * n:128 * n + m]).then_inc(pt_ok, 1)
            dve.wait_ge(sgt_ps, 1)
            dve.tensor_copy(SGT.rearrange("p a b -> p (a b)"), X1[:]).then_inc(sgt_ok, 1)

            def ada(n):
                at = item_at("a", n)
                wait_item(dve, at)
                if n == 0:
                    dve.wait_ge(ca_ok, 1)
                    dve.wait_ge(pt_ok, 4)
                if n >= 2:
                    dve.wait_ge(red, n - 1)
                acc, w = ACC[n % 2], slot(at)
                link(dve.tensor_scalar(acc, w[:, 0, :], CA[:, 0:1], None, ALU.mult))
                for k in range(1, KC):
                    ins = dve.scalar_tensor_tensor(out=acc, in0=w[:, k, :], scalar=CA[:, k:k + 1],
                                                   in1=acc, op0=ALU.mult, op1=ALU.add)
                    if k < KC - 1:
                        link(ins)
                ins.then_inc(ada_used, 1)

            def ada_finish(n):
                l, s, h = n // 24, (n % 24) // 4, n % 4
                dve.wait_ge(red, n + 1)
                if s in (2, 5):
                    q = (2 * l + s // 3) * 4 + h
                    dve.wait_ge(brow_in[q % 2], 16 * (q // 2 + 1))
                    tt(BROW[q % 2], X0[0:1, 0:QW], BROW[q % 2], ALU.add).then_inc(ada_fin, 1)
                    return
                o = MC[:, l, 2 * (s // 3) + (1 - s % 3), 2 * h:2 * h + 2]
                c0 = COL_ADAB + 48 * l + 8 * s + 2 * h
                if s % 3 == 0:
                    tt(o, X0[:, 0:2], PT[:, c0:c0 + 2], ALU.add).then_inc(ada_fin, 1)
                else:
                    link(tt(o, X0[:, 0:2], PT[:, c0:c0 + 2], ALU.add))
                    g0 = (COL_NMIX if s == 1 else COL_NFFN) + 8 * l + 2 * h
                    dve.scalar_tensor_tensor(out=o, in0=o, scalar=1.0, in1=PT[:, g0:g0 + 2],
                                             op0=ALU.add, op1=ALU.mult).then_inc(ada_fin, 1)

            def beside(wn, n, evict=None):
                if n < len(BESIDE[wn]):
                    ada(BESIDE[wn][n])
                if evict is not None:
                    evict()
                if n < len(BESIDE[wn]):
                    ada_finish(BESIDE[wn][n])

            def rms_apply(r):
                for h in range(NH):
                    dve.wait_ge(rms_sd, 2 * r + h + 1)
                    s = slice(4 * h, 4 * h + 4)
                    link(dve.reciprocal(RSTD[:, s], SD[:, s]))
                    if r == 4:
                        for b in range(4 * h, 4 * h + 4):
                            if b == 0:
                                dve.wait_ge(small_in, 48)
                            if b >= 4:
                                dve.wait_ge(o_out[b % 4], 16)
                            dve.scalar_tensor_tensor(out=OUTS[b % 4], in0=X[:, b, :],
                                                     scalar=RSTD[:, b:b + 1], in1=FGB, op0=ALU.mult,
                                                     op1=ALU.mult).then_inc(out_ok, 1)
                        continue
                    for b in range(4):
                        dve.tensor_scalar(XN[h][:, b, :], X[:, 4 * h + b, :],
                                          RSTD[:, 4 * h + b:4 * h + b + 1], None,
                                          ALU.mult).then_inc(xn_ok, 1)

            def evict_ht(r, l, ffn):
                dve.wait_ge(ada_fin, NADA if r else NADA0)
                for h in range(NH):
                    for k in range(1, KC, 2):
                        dve.wait_ge(tr, 16 * r + 8 * h + k + 1)
                        dve.tensor_scalar(HTR[:, k, HT * h:HT * h + HT], TB_[1][:],
                                          MC[:, l, 2 * ffn, k:k + 1], MC[:, l, 2 * ffn + 1, k:k + 1],
                                          ALU.mult, ALU.add).then_inc(tev_d, 1)

            def rms_and_evict(r, l, ffn):
                rms_apply(r)
                evict_ht(r, l, ffn)

            def take(g):
                dve.wait_ge(full, g + 1)
                return M[g % 4]

            def first_max(o_oh, src, tmp, red1, pri):
                shape = list(src.shape)
                link(dve.tensor_reduce(red1, src, AX.X, ALU.max))
                link(tt(tmp, src, red1.unsqueeze(len(shape) - 1).broadcast_to(shape), ALU.is_equal))
                link(tt(tmp, tmp, pri, ALU.mult))
                link(dve.tensor_reduce(red1, tmp, AX.X, ALU.max))
                link(tt(o_oh, tmp, red1.unsqueeze(len(shape) - 1).broadcast_to(shape), ALU.is_equal))

            def route(l):
                full3 = [P, NB, NE]
                g4 = [P, NB * NG, EG]

                def grp(a):
                    return a.rearrange("p a b -> p (a b)").rearrange("p (g e) -> p g e", e=EG)
                dve.wait_ge(sco_ok, l + 1)
                link(tt(BIA, SCO, RB[:].unsqueeze(1).broadcast_to(full3), ALU.add))
                link(dve.tensor_scalar(PRI, IOTA[:, 0:NE].unsqueeze(1).broadcast_to(full3), -1.0,
                                       float(NE), ALU.mult, ALU.add))
                b4 = grp(BIA)
                pa = R[:, 3, 10 * ne:10 * ne + 6 * NB * NG].rearrange("p (g e) -> p g e", e=6)
                tt(pa[:, :, 0:3], b4[:, :, 0:3], b4[:, :, 1:4], ALU.add)
                tt(pa[:, :, 3:5], b4[:, :, 0:2], b4[:, :, 2:4], ALU.add)
                link(tt(pa[:, :, 5:6], b4[:, :, 0:1], b4[:, :, 3:4], ALU.add))
                gs = SM[:, 0:32]
                link(dve.tensor_reduce(gs, pa, AX.X, ALU.max))
                gs3 = gs.rearrange("p (b g) -> p b g", g=NG)
                sel = SM[:, 32:64].rearrange("p (b g) -> p b g", g=NG)
                tmp = SM[:, 64:96].rearrange("p (b g) -> p b g", g=NG)
                one = SM[:, 96:104]
                first_max(sel, gs3, tmp, one, PRI[:, :, 0:NG])
                selb = SM[:, 32:64].unsqueeze(2).broadcast_to(g4)
                link(tt(grp(TA), grp(BIA), selb, ALU.mult))
                link(dve.tensor_scalar(grp(TB), selb, -1.0, BIG, ALU.add, ALU.mult))
                link(tt(MSK, TA, TB, ALU.add))
                first_max(OH1, MSK, TA, one, PRI)
                link(dve.scalar_tensor_tensor(out=MSK, in0=OH1, scalar=-2.0 * BIG, in1=MSK,
                                              op0=ALU.mult, op1=ALU.add))
                first_max(OH2, MSK, TA, one, PRI)
                tt(MM, OH1, OH2, ALU.add).then_inc(mm_ok, 1)
                s1, s2, ssum = SM[:, 0:8], SM[:, 8:16], SM[:, 16:24]
                link(tt(TA, SCO, OH1, ALU.mult))
                link(dve.tensor_reduce(s1, TA, AX.X, ALU.add))
                link(tt(TB, SCO, OH2, ALU.mult))
                link(dve.tensor_reduce(s2, TB, AX.X, ALU.add))
                link(tt(ssum, s1, s2, ALU.add))
                link(dve.reciprocal(ssum, ssum))
                tt(GATE[:, 0, :], s1, ssum, ALU.mult)
                link(tt(GATE[:, 1, :], s2, ssum, ALU.mult))
                dve.wait_ge(cnt, l + 1)
                link(dve.tensor_copy(TA.rearrange("p a b -> p (a b)"), X1[:, 0:ne]))
                base = SM[:, 32:48]
                link(dve.tensor_copy(base, X1[:, ne:ne + NE]))
                for b in range(1, NB):
                    link(tt(TA[:, b, :], TA[:, b, :], base, ALU.add))
                    link(tt(base, base, X1[:, ne + NE * b:ne + NE * b + NE], ALU.add))
                j7 = R[:, 3, 10 * ne:10 * ne + 7 * NE].rearrange("p (e j) -> p e j", j=7)
                link(dve.tensor_scalar(j7, IOTA[:, 1:8].unsqueeze(1).broadcast_to([P, NE, 7]),
                                       float(P), None, ALU.mult))
                link(tt(j7, base.unsqueeze(2).broadcast_to([P, NE, 7]), j7, ALU.is_gt))
                ntl, ca, cb = SM[:, 48:64], SM[:, 64:80], SM[:, 80:96]
                link(dve.tensor_reduce(ntl, j7, AX.X, ALU.add))
                link(dve.tensor_scalar(ntl, ntl, 1.0, None, ALU.add))
                link(dve.tensor_copy(ca, ntl))
                for s in (1, 2, 4, 8):
                    dve.tensor_copy(cb[:, 0:s], ca[:, 0:s])
                    link(tt(cb[:, s:NE], ca[:, s:NE], ca[:, 0:NE - s], ALU.add))
                    ca, cb = cb, ca
                inc = ca
                off = SM[:, 96:112]
                link(tt(off, inc, ntl, ALU.subtract))
                link(dve.tensor_scalar(off, off, float(P), None, ALU.mult))
                link(tt(TA, TA, off.unsqueeze(1).broadcast_to(full3), ALU.add))
                for s, oh in ((0, OH1), (1, OH2)):
                    link(tt(TB, TA, oh, ALU.mult))
                    link(dve.tensor_reduce(SLOTF[:, s, :], TB, AX.X, ALU.add))
                link(dve.tensor_copy(SLOTU[:], SLOTF[:]))
                si = SM[:, 0:16].bitcast(I32)
                sj = SM[:, 16:32].bitcast(I32)
                slf = SLOTF[:].rearrange("p a b -> p (a b)")
                link(dve.tensor_copy(si, slf))
                link(dve.tensor_scalar(sj, si, 7, None, ALU.arith_shift_right))
                qf, rf = SM[:, 32:48], SM[:, 112:128]
                link(dve.tensor_copy(qf, sj))
                link(dve.scalar_tensor_tensor(out=rf, in0=qf, scalar=-float(P), in1=slf,
                                              op0=ALU.mult, op1=ALU.add))
                q3 = [P, 16, MAXT]
                link(tt(QO, IOTA[:, 0:MAXT].unsqueeze(1).broadcast_to(q3),
                        qf.unsqueeze(2).broadcast_to(q3), ALU.is_equal))
                q4 = QO.rearrange("p (s b) q -> p s b q", s=TOPK)
                for s in range(TOPK):
                    tt(q4[:, s], q4[:, s], TOKF[:].unsqueeze(2).broadcast_to([P, NB, MAXT]), ALU.mult)
                tt(RO, IOTA[:].unsqueeze(1).broadcast_to([P, 16, P]),
                   rf.unsqueeze(2).broadcast_to([P, 16, P]), ALU.is_equal).then_inc(oh_ok, 1)
                rowt = R[0:1, 3, 0:MAXT * NE].rearrange("p (t e) -> p t e", e=NE)
                ex = ROWT[:, 0:MAXT]
                sh = [1, MAXT, NE]
                link(tt(rowt, inc[0:1].unsqueeze(1).broadcast_to(sh),
                        IOTA[0:1, 0:MAXT].unsqueeze(2).broadcast_to(sh), ALU.is_le))
                link(dve.tensor_reduce(ex, rowt, AX.X, ALU.add))
                dve.tensor_copy(RTF[:, 0:1], inc[0:1, NE - 1:NE])
                dve.tensor_copy(RTF[:, 1 + NE:MAXT], IOTA[0:1, 1 + NE:MAXT])
                link(dve.tensor_copy(RTF[:, 1:1 + NE], inc[0:1]))
                sh6 = [1, MAXT, 6]
                row6 = R[0:1, 3, 0:MAXT * 6].rearrange("p (t e) -> p t e", e=6)
                for b in range(NEB):
                    th = ROWT[:, MAXT:MAXT + 6]
                    link(dve.tensor_scalar(th, IOTA[0:1, 0:6], float(NEB), float(b), ALU.mult, ALU.add))
                    link(tt(row6, th.unsqueeze(1).broadcast_to(sh6), ex.unsqueeze(2).broadcast_to(sh6),
                            ALU.is_le))
                    link(dve.tensor_reduce(ROWT[:, (2 + b) * MAXT:(3 + b) * MAXT], row6, AX.X, ALU.add))
                    link(dve.tensor_scalar(RTF[:, (1 + b) * MAXT:(2 + b) * MAXT],
                                           ROWT[:, (2 + b) * MAXT:(3 + b) * MAXT], 48.0, None, ALU.mult))
                bf = ROWT[:, 5 * MAXT:6 * MAXT]
                link(dve.scalar_tensor_tensor(out=bf, in0=ROWT[:, 2 * MAXT:3 * MAXT],
                                              scalar=-float(NEB), in1=ex, op0=ALU.mult, op1=ALU.add))
                link(dve.tensor_scalar(RTF[:, 4 * MAXT:5 * MAXT], bf, float(NEB), float(EXP),
                                       ALU.add, ALU.mult))
                link(dve.tensor_copy(RT[:], RTF[:]))
                dve.wait_ge(tok_ps, l + 1)
                dve.tensor_copy(TOKI[:], X0[:, 0:MAXT]).then_inc(tab_ok, 1)

            def experts(l):
                nt = dve.value_load(RT[0:1, 0:1], min_val=1, max_val=MOST)

                def evict_tile(n_tr):
                    dve.wait_ge(xtr[l], n_tr)
                    for k in range(4, KC):
                        ins = dve.tensor_scalar(XT[:, k, :], TB_[1][:, (k - 4) * P:(k - 3) * P],
                                                MC[:, l, 2, k:k + 1], MC[:, l, 3, k:k + 1],
                                                ALU.mult, ALU.add)
                    ins.then_inc(xt_d[l], 1)
                evict_tile(1)
                dve.sem_inc(ys_d[l], 1)
                with dve.Fori(0, nt) as t:
                    dve.wait_ge(gu[l], t + 1)
                    dve.wait_ge(sg_ok[l], t + 1)
                    tt(AG, M[0][:, FE:2 * FE], SG, ALU.mult).then_inc(ag_ok[l], 1)
                    dve.wait_ge(atr[l], t + 1)
                    dve.tensor_copy(AT.rearrange("p a b -> p (a b)"), X0[:, 0:FE]).then_inc(at_ok[l], 1)
                    evict_tile(t + 2)
                    dve.wait_ge(dn[l], t + 1)
                    dve.wait_ge(y_out[l], t * 16 + 16)
                    dve.tensor_copy(YS[:, HT:D], M[2][:]).then_inc(ys_d[l], 1)
                for b in range(NB):
                    dve.wait_ge(c_in[l][b % 2][1], 16 * (b // 2 + 1))
                    dve.wait_ge(ym_ok, l * NB + b + 1)
                    if b == 0:
                        dve.wait_ge(gb_in[2 * l + 1], 16)
                    y = Y2[b % 2]
                    link(dve.scalar_tensor_tensor(out=y, in0=y, scalar=GATE[:, 1, b:b + 1],
                                                  in1=YM[b % 2], op0=ALU.mult, op1=ALU.add))
                    link(tt(y, y, GBF, ALU.mult))
                    tt(X[:, b, :], X[:, b, :], y, ALU.add).then_inc(xup, 1)

            def add_out(g, n, gb, tmp, b2=None):
                c = QW * (n // 4)
                b = 2 * (n % 4)
                sh = [P, 2, QW]
                t = tmp[n % 2].rearrange("p (b c) -> p b c", b=2)
                ps = take(g)[:].rearrange("p (b c) -> p b c", b=2)
                gate = gb[:, c:c + QW].unsqueeze(1).broadcast_to(sh)
                bias = None if b2 is None else b2[:, c:c + QW].unsqueeze(1).broadcast_to(sh)
                if b2 is None:
                    tt(t, ps, gate, ALU.mult).then_inc(free["D"], 1)
                    dve.wait_ge(free["D"], emptied(g))
                else:
                    tt(t, ps, bias, ALU.add).then_inc(free["D"], 1)
                    dve.wait_ge(free["D"], emptied(g))
                    link(tt(t, t, gate, ALU.mult))
                x = X[:, b:b + 2, c:c + QW]
                ins = tt(x, x, t, ALU.add)
                if n >= 12:
                    ins.then_inc(xup, 2)

            for n in range(NADA0):
                ada(n)
                ada_finish(n)
            rms_and_evict(0, 0, 0)
            for n in range(8):
                beside(WV + n // 4, n % 4)
            dve.wait_ge(sgu_in, 64)
            for b in range(NB):
                dve.wait_ge(free["A"], emptied(GROUPS["v"] + 4 + b // 2))
                link(dve.bn_stats(BST[:, b, :], V[:, b, :]))
                ins = dve.bn_aggr(MV[:, b, :], BST[:, b, :])
            ins.then_inc(ln_var, 1)
            dve.wait_ge(ln_var, 1)
            dve.wait_ge(ln_sd, 1)
            link(dve.reciprocal(RSTD[:], SD[:]))
            for b in range(NB):
                v = V[:, b, :]
                link(dve.tensor_scalar(v, v, MV[:, b, 0:1], RSTD[:, b:b + 1], ALU.subtract, ALU.mult))
                link(tt(v, v, LNG, ALU.mult))
                tt(v, v, LNB, ALU.add).then_inc(v_ok, 1)
            for n in range(8):
                beside(WCG + n // 4, n % 4)
            for n in range(8):
                hd, h = n // 2, n % 2
                o = YC[:, hd, HT * h:HT * h + HT].rearrange("p (c t) -> p c t", t=P)
                tt(o, take(GROUPS["sgu"] + n)[:].rearrange("p (c t) -> p c t", t=P),
                   SBB[:, hd, :].unsqueeze(1).broadcast_to([P, 4, P]), ALU.add).then_inc(free["D"], 1)
            dve.wait_ge(free["A"], emptied(GROUPS["cg"] + 7))
            for n in range(8):
                c, h = n // 2, n % 2
                g = GROUPS["hb"] + n
                s = slice(HT * h, HT * h + HT)
                beside(WHB + n // 4, n % 4,
                       lambda: tt(PB[:, c, s], PB[:, c, s], take(g)[:], ALU.mult).then_inc(free["D"], 1))
                if h == 0:
                    continue
                dve.wait_ge(free["D"], emptied(g))
                o, p = YC[:, 4 + c, :], PB[:, c, :]

                def tap(j):
                    return PT[:, COL_SC + 4 * j + c:COL_SC + 4 * j + c + 1]
                link(dve.tensor_scalar(o, p, tap(BTAPS - 1), None, ALU.mult))
                for j in range(BTAPS - 2, -1, -1):
                    d = BTAPS - 1 - j
                    link(dve.scalar_tensor_tensor(out=o[:, d:T], in0=p[:, 0:T - d], scalar=tap(j),
                                                  in1=o[:, d:T], op0=ALU.mult, op1=ALU.add))
            for n in range(8):
                c, h = n // 2, n % 2
                o = YC[:, 4 + c, HT * h:HT * h + HT]
                g = GROUPS["bg"] + n
                beside(WBG + n // 4, n % 4,
                       lambda: tt(o, o, take(g)[:], ALU.mult).then_inc(free["D"], 1))
            for n in range(8):
                c, h = n // 2, n % 2
                o = YC[:, c, HT * h:HT * h + HT]

                def gate():
                    dve.wait_ge(free["A"], emptied(GROUPS["u"] + n))
                    tt(o, o, GU[n % 2], ALU.mult).then_inc(ya_ok, 1)
                beside(WU + n // 4, n % 4, gate)
            dve.wait_ge(gb_in[0], 16)
            for n in range(16):
                beside(WWO + n // 4, n % 4, lambda: add_out(GROUPS["wo"] + n, n, GB0, TMPO))
            rms_and_evict(1, 0, 1)
            route(0)
            experts(0)
            rms_and_evict(2, 1, 0)
            for c in range(KC):
                for h in range(NH):
                    g = GROUPS["w1"] + 4 * c + 2 * h + 1
                    dve.wait_ge(free["A"], emptied(g - 1))
                    dve.scalar_tensor_tensor(out=GT[:, c, HT * h:HT * h + HT], in0=take(g)[:],
                                             scalar=PT[:, COL_B1 + c:COL_B1 + c + 1],
                                             in1=SIG[h], op0=ALU.add, op1=ALU.mult).then_inc(free["D"], 1)
                dve.wait_ge(free["D"], emptied(g))
                o, p = CV[:, c, :], GT[:, c, :]

                def tap(j):
                    return PT[:, COL_DW + KC * j + c:COL_DW + KC * j + c + 1]
                link(dve.tensor_scalar(o, p, tap(CTAPS - 1), PT[:, COL_DWB + c:COL_DWB + c + 1],
                                       ALU.mult, ALU.add))
                for j in range(CTAPS - 2, -1, -1):
                    d = CTAPS - 1 - j
                    ins = dve.scalar_tensor_tensor(out=o[:, d:T], in0=p[:, 0:T - d], scalar=tap(j),
                                                   in1=o[:, d:T], op0=ALU.mult, op1=ALU.add)
                    if j:
                        link(ins)
                ins.then_inc(conv_ok, 1)
            dve.wait_ge(conv_ok, KC)
            for h in range(NH):
                s = slice(HT * h, HT * h + HT)
                g = GROUPS["mu"] + h
                dve.tensor_scalar(MUB[h], take(g)[:], 1.0 / D, None, ALU.mult).then_inc(free["D"], 1)
                dve.wait_ge(free["D"], emptied(g))
                for k in range(KC):
                    tt(CV[:, k, s], CV[:, k, s], MUB[h], ALU.subtract).then_inc(cen_ok, 1)
            for h in range(NH):
                s = slice(HT * h, HT * h + HT)
                dve.wait_ge(free["A"], emptied(GROUPS["var"] + h))
                link(dve.reciprocal(RSB[h], RSB[h]))
                dve.wait_ge(cen_ok, KC * h + KC)
                for k in range(KC):
                    tt(CV[:, k, s], CV[:, k, s], RSB[h], ALU.mult).then_inc(nrm_ok, 1)
            dve.wait_ge(gb_in[2], 32)
            for n in range(16):
                add_out(GROUPS["w2"] + n, n, GB1, TMP1, B2B)
            rms_and_evict(3, 1, 1)
            route(1)
            experts(1)
            rms_apply(4)


INPUTS = ["x", "c", "ada_w", "ada_b", "norm_mix_g", "norm_ffn_g", "hyb_w_in", "sgu_ln_g", "sgu_ln_b",
          "sgu_w", "sgu_b", "sconv_w", "hyb_w_out", "conf_w1", "conf_b1", "conf_dw_w", "conf_dw_b",
          "conf_ln_g", "conf_ln_b", "conf_w2", "conf_b2", "router_w", "router_bias", "moe_w_gate",
          "moe_w_up", "moe_w_down", "final_norm_g"]


def kernel(**inputs):
    import concourse.bacc as bacc
    from concourse.bass_utils import run_bass_kernel_spmd

    nc = bacc.Bacc("TRN2", target_bir_lowering=False, num_devices=1)
    arrays, aps = {}, {}
    for name in INPUTS:
        a = np.ascontiguousarray(inputs[name])
        arrays[f"in_{name}"] = a
        aps[name] = nc.dram_tensor(f"in_{name}", a.shape, mybir.dt.from_np(a.dtype),
                                   kind="ExternalInput").ap()
    out = nc.dram_tensor("out", (1, T, D), F32, kind="ExternalOutput").ap()
    trunk(nc, aps, out)
    r = run_bass_kernel_spmd(nc, [arrays], core_ids=[0])
    return r.results[0]["out"]
```

```python
from contextlib import ExitStack

import numpy as np

import concourse.bass as bass
from concourse import mybir

F32 = mybir.dt.float32
I32 = mybir.dt.int32
U32 = mybir.dt.uint32
ALU = mybir.AluOpType
ACT = mybir.ActivationFunctionType
AX = mybir.AxisListType

P = 128
D = 1024
T = 1024
KC = D // P
NB = T // P
NL = 2
HT = 512
NH = 2
DA = 512
HEADS = 4
NE = 16
NG = 4
EG = NE // NG
FE = 256
TOPK = 2
CTAPS = 31
BTAPS = 3
LEAST = T * TOPK // P
MOST = LEAST + NE - 1
MAXT = MOST + 1
EPS = 1e-6
BIG = 1e30

COL_ADAB, COL_NMIX, COL_NFFN = 0, 96, 112
COL_SC, COL_B1, COL_DWB, COL_LNG, COL_LNB, COL_C = 128, 140, 156, 164, 172, 180
COL_DW = 188
NTAB_B = 60
NDW = CTAPS * KC
NPT = COL_DW + NDW

QW = 256
NADA = NL * 6 * D // QW
NADA0 = 2 * D // QW
WV, WCG, WHB, WBG, WU, WWO, NW0 = 0, 2, 4, 6, 8, 10, 14
BESIDE = []
_n = NADA0
for _w in range(NW0):
    _k = {WV: 4, WV + 1: 4, WHB: 5, WHB + 1: 5, WBG: 5, WBG + 1: 5, WU: 4, WU + 1: 4, NW0 - 1: 4}.get(_w, 0)
    BESIDE.append(list(range(_n, _n + _k)))
    _n += _k
ITEMS = [("a", n) for n in range(NADA0)]
for _w in range(NW0):
    ITEMS += [("w", _w)] + [("a", n) for n in BESIDE[_w]]
NSLOT = 8
SLOT = KC * QW
EXP = KC * 2 * FE + 2 * D
NEB = 3
ITEM0 = len(ITEMS)
NSLOT1 = 7
NW1 = 12
PTAPS = [5, 5, 5, 5, 5, 5, 5, 8]
MAXP = max(PTAPS)

GROUPS = {}
CONSUMER = []
for _name, _who in (("v", "A" * 8), ("cg", "A" * 8), ("sgu", "D" * 8), ("hb", "D" * 8),
                    ("bg", "D" * 8), ("u", "A" * 8), ("wo", "D" * 16), ("w1", "AD" * 16),
                    ("var", "A" * 2), ("w2", "D" * 16)):
    GROUPS[_name] = len(CONSUMER)
    CONSUMER += list(_who)


USED0 = [GROUPS[_g] + 4 * (_j + 1) for _g in ("v", "cg", "hb", "bg", "u") for _j in range(2)]
USED0 += [GROUPS["wo"] + 16] * 4
USED1 = ([GROUPS["w1"] + 8 * (_j // 2 + 1) for _j in range(8)]
         + [GROUPS["w2"] + 16] * 4)


def beside_of(wn, n):
    a = BESIDE[wn]
    return a[n * len(a) // 4:(n + 1) * len(a) // 4]


def beside_out(p, j):
    return BESIDE[-1][2 * p + j // 2] if p < 2 and j % 2 == 0 else None


def emptied(g):
    return CONSUMER[:g + 1].count(CONSUMER[g])


def trunk(nc, i, out):
    with ExitStack() as ctx:
        def sb(name, shape, dt=F32):
            return ctx.enter_context(nc.sbuf_tensor(name, shape, dt))

        def sem(name):
            return ctx.enter_context(nc.semaphore(name))

        X = sb("X", [P, NB, D])
        HTR = sb("HTR", [P, KC, T])
        R = sb("R", [P, 4, NB * DA])
        W = sb("W", [P, NEB * EXP])
        PT = sb("PT", [P, NPT])
        MC = sb("MC", [P, NL, 4, KC])
        IDENT = sb("IDENT", [P, P])
        ONES = sb("ONES", [P, P])
        TRI = sb("TRI", [P, P])
        IOTA = sb("IOTA", [P, P])
        RW = sb("RW", [P, KC, NE])
        RB = sb("RB", [P, NE])
        CA = sb("CA", [P, KC])
        EPSC = sb("EPSC", [P, 1])
        SS = sb("SS", [P, NB])
        SD = sb("SD", [P, NB])
        RSTD = sb("RSTD", [P, NB])
        GATE = sb("GATE", [P, TOPK, NB])
        GSLOT = sb("GSLOT", [P, MAXT])
        SLOTF = sb("SLOTF", [P, TOPK, NB])
        SLOTU = sb("SLOTU", [P, TOPK, NB], U32)
        TOKI = sb("TOKI", [P, MAXT], U32)
        TCUR = sb("TCUR", [P, 1], U32)
        RT = sb("RT", [1, 5 * MAXT], I32)
        RTF = sb("RTF", [1, 5 * MAXT])
        PSCR = sb("PSCR", [1, 3])
        WT = sb("WT", [P, 8])

        def slot(n, of=NSLOT):
            return W[:, (n % of) * SLOT:(n % of + 1) * SLOT].rearrange("p (k n) -> p k n", k=KC)
        slack = NSLOT * SLOT
        ACC = [W[:, slack + b * QW:slack + (b + 1) * QW] for b in range(2)]
        NBROW = 4
        BROW = [W[0:1, slack + (2 + b) * QW:slack + (3 + b) * QW] for b in range(NBROW)]
        SIG = [W[:, slack + (1 + b) * HT:slack + (2 + b) * HT] for b in range(2)]

        DIAG = [W[:, NSLOT1 * SLOT + b * MAXP * P:NSLOT1 * SLOT + (b + 1) * MAXP * P].rearrange(
            "p (j c) -> p j c", j=MAXP) for b in range(2)]
        ZERO = W[:, slack + 3 * HT:slack + 4 * HT]

        def r3(n, a):
            return R[:, n, :].rearrange("p (a b) -> p a b", a=a)
        XN = [r3(0, 4), r3(2, 4)]
        V = r3(0, NB)
        PB = r3(1, 4)
        YC = R[:, 2:4, :].rearrange("p r (c t) -> p (r c) t", t=T)
        TABS = R[:, 1, 0:4 * P].rearrange("p (a b) -> p a b", a=4)
        SGW = R[:, 3, 0:HT].rearrange("p (a b) -> p a b", a=HEADS)
        SGT = R[:, 3, HT:2 * HT].rearrange("p (a b) -> p a b", a=HEADS)
        LNG = R[:, 3, 2 * HT:3 * HT]
        LNB = R[:, 3, 3 * HT:4 * HT]
        SBB = R[:, 3, 4 * HT:5 * HT].rearrange("p (a b) -> p a b", a=HEADS)
        BST = R[:, 3, 5 * HT:5 * HT + 6 * NB].rearrange("p (a b) -> p a b", b=6)
        MV = R[:, 3, 5 * HT + 64:5 * HT + 64 + 2 * NB].rearrange("p (a b) -> p a b", b=2)
        GU = [R[:, 0, b * HT:(b + 1) * HT] for b in range(2)]
        GB0 = R[:, 1, 2 * HT:4 * HT]
        TMPO = [R[:, 1, b * HT:(b + 1) * HT] for b in range(2)]
        GT = R[:, 0:2, :].rearrange("p r (c t) -> p (r c) t", t=T)
        CV = YC
        MUB = [R[:, 0, b * HT:(b + 1) * HT] for b in range(2)]
        SQ = [R[:, 0, (2 + b) * HT:(3 + b) * HT] for b in range(2)]
        RSB = [R[:, 0, (4 + b) * HT:(5 + b) * HT] for b in range(2)]
        GB1 = R[:, 1, 0:D]
        B2B = R[:, 1, D:2 * D]
        TMP1 = [R[:, 1, 2 * D + b * HT:2 * D + (b + 1) * HT] for b in range(2)]
        XG = R[:, 1, 0:D]
        XT = R[:, 1, D:2 * D].rearrange("p (k t) -> p k t", k=KC)
        YS = R[:, 1, 2 * D:3 * D]
        SG = R[:, 1, 3 * D:3 * D + FE]
        AG = R[:, 1, 3 * D + FE:3 * D + 2 * FE]
        AT = R[:, 1, 3 * D + 2 * FE:3 * D + 3 * FE].rearrange("p (k t) -> p k t", k=2)
        JUNK = R[:, 1, 3 * D:4 * D]
        ne = NB * NE

        def rt(n, a=NB):
            return R[:, 3, n * ne:(n + 1) * ne].rearrange("p (a b) -> p a b", a=a)
        SCO, BIA, MSK, OH1, OH2, MM, TA, TB, PRI = (rt(n) for n in range(9))
        SM = R[:, 3, 9 * ne:10 * ne]
        QQ = HTR[:, 0, :].rearrange("p (n a b) -> p n a b", a=2, b=MAXT)
        QO, QG = QQ[:, :, 0, :], QQ[:, :, 1, :]
        SCT = HTR[0:NE, 1, :]
        RO = R[:, 3, 14 * ne:30 * ne].rearrange("p (a b) -> p a b", b=P)
        ROWT = R[0:1, 3, 30 * ne:30 * ne + 2 * P]
        TOKF = WT
        def hv(n):
            return HTR[:, n, :]
        Y1, Y2 = ([HTR[:, 3 * n + b, :] for b in range(3)] + [R[:, 3 - n, b * D:(b + 1) * D] for b in range(4)]
                  for n in range(2))
        NY0, NY = 3, 7

        def y_of(b):
            return b if b < NY else NY0
        GBF = hv(6)
        FGB = hv(7)
        OUTS = [XN[b // 4][:, b % 4, :] for b in range(NB)]

        bank = [ctx.enter_context(nc.psum_tensor(f"bank{n}", [P, HT], F32)) for n in range(8)]
        M = bank[0:4]
        TB_ = bank[4:6]
        X0, X1 = bank[6], bank[7]

        xn_dram = nc.dram_tensor("xn_scratch", (T, D), F32, kind="Internal").ap()
        y_dram = nc.dram_tensor("y_scratch", (MOST * P, D), F32, kind="Internal").ap()
        g_dram = nc.dram_tensor("gate_scratch", (4, D), F32, kind="Internal").ap()

        xl = [sem(f"x_loaded{n}") for n in range(2)]
        tabs_in = sem("table_rows_loaded")
        small_in = sem("small_params_loaded")
        sgu_in = sem("sgu_params_loaded")
        const = sem("constants_made")
        pt_ps = sem("param_transpose_done")
        pt_ok = sem("param_columns_ready")
        ca_ok = sem("c_act_ready")
        sgw_ok = sem("sgu_w_masked")
        sgt_ps = sem("sgu_w_transposed")
        sgt_ok = sem("sgu_w_columns_ready")
        ring = [sem(f"ring_slot_loaded{n}") for n in range(NSLOT)]
        ada_used = sem("ada_group_summed")
        red = sem("ada_reduced")
        ada_fin = sem("ada_finished")
        brow_out = [sem(f"gate_row_stored{n}") for n in range(NBROW)]
        zeroed = sem("scratch_rows_zeroed")
        rms_sd = sem("rms_root_ready")
        xn_ok = sem("xn_ready")
        xn_out = [sem(f"xn_stored{n}") for n in range(2)]
        tr = sem("xn_transposed")
        tev_a = sem("ht_evicted_by_act")
        tev_d = sem("ht_evicted_by_dve")
        full = sem("main_bank_full")
        free = {"A": sem("main_bank_emptied_by_act"), "D": sem("main_bank_emptied_by_dve")}
        ln_var = sem("ln_variance_ready")
        ln_sd = sem("ln_root_ready")
        v_ok = sem("v_normed")
        ya_ok = sem("head_a_output_ready")
        gb_in = [sem(f"gate_rows_in{n}") for n in range(4)]
        xup = sem("x_updated")
        dch = sem("dve_step")
        act_ch = sem("act_step")
        conv_ok = sem("conv_ready")
        cen_ok = sem("centred")
        sq1_ok = sem("squares_ready")
        sq1_used = sem("squares_used")
        nrm_ok = sem("normalised")
        z_ok = sem("z_ready")
        lg = sem("logits_done")
        sco_ok = sem("scores_ready")
        sct_ok = sem("scores_by_expert_ready")
        sct_tr = sem("scores_transposed")
        mm_ok = sem("choice_mask_ready")
        cnt = sem("counts_done")
        oh_ok = sem("slot_one_hots_ready")
        tok_ps = sem("slot_tokens_done")
        tab_ok = sem("tables_ready")
        e_in = [[sem(f"expert_loaded{l}_{b}") for b in range(NEB)] for l in range(NL)]
        xg_in = [sem(f"tile_gathered{l}") for l in range(NL)]
        cur_ok = [sem(f"tile_tokens_copied{l}") for l in range(NL)]
        held = [sem(f"gather_waits_met{l}") for l in range(NL)]
        xtr = [sem(f"tile_transposed{l}") for l in range(NL)]
        xt_a = [sem(f"tile_evicted_by_act{l}") for l in range(NL)]
        xt_d = [sem(f"tile_evicted_by_dve{l}") for l in range(NL)]
        gu = [sem(f"gate_up_done{l}") for l in range(NL)]
        sg_ok = [sem(f"silu_ready{l}") for l in range(NL)]
        ag_ok = [sem(f"hidden_ready{l}") for l in range(NL)]
        atr = [sem(f"hidden_transposed{l}") for l in range(NL)]
        at_ok = [sem(f"hidden_columns_ready{l}") for l in range(NL)]
        dn = [sem(f"down_done{l}") for l in range(NL)]
        ys_d = [sem(f"tile_out_ready{l}") for l in range(NL)]
        y_out = [sem(f"tile_stored{l}") for l in range(NL)]
        c_in = [[[sem(f"combine_in{l}_{b}_{s}") for s in range(2)] for b in range(NB)] for l in range(NL)]
        out_ok = sem("output_block_ready")
        o_out = sem("output_stored")
        diag_ok = sem("diagonals_ready")
        cv_ps = sem("conv_taps_summed")
        mu_ps = sem("mean_summed")

        def cols(w, c0):
            return w.rearrange("(k p) n -> p k n", p=P)[:, :, c0:c0 + QW]
        w_in, w_out = i["hyb_w_in"][0], i["hyb_w_out"][0]
        W0 = [cols(w_in, sec * DA + h * QW) for sec in (1, 3, 4, 2, 0) for h in range(2)]
        W0 += [cols(w_out, h * QW) for h in range(4)]
        w1, w2 = i["conf_w1"][0], i["conf_w2"][0]
        W1 = [cols(w1, part * D + h * QW) for h in range(4) for part in (1, 0)]
        W1 += [cols(w2, h * QW) for h in range(4)]
        x_rows = i["x"][0].rearrange("(b p) d -> p b d", p=P)
        out_rows = out[0].rearrange("(b p) d -> p b d", p=P)
        rows = {n: i[n].rearrange("a (r q) -> (a r) q", q=P)
                for n in ("ada_b", "norm_mix_g", "norm_ffn_g", "conf_b1", "conf_dw_b", "conf_ln_g",
                          "conf_ln_b", "c")}
        rows["sconv"] = i["sconv_w"][0].rearrange("j (r q) -> (j r) q", q=P)
        rows["dw"] = i["conf_dw_w"][0].rearrange("j (r q) -> (j r) q", q=P)

        def on_all(v, n):
            return v.rearrange("(a n) -> a n", a=1).broadcast_to([P, n])

        def item_at(kind, n):
            return ITEMS.index((kind, n))

        def wait_item(eng, at):
            eng.wait_ge(ring[at % NSLOT], 16 * (at // NSLOT + 1))

        def wait_used(eng, at):
            kind, n = ITEMS[at]
            if kind == "a":
                eng.wait_ge(ada_used, n + 1)
            else:
                eng.wait_ge(full, USED0[n])

        def w1_group(n):
            return (n % 2, n // 2) if n < 4 else (n // 2, n % 2)

        block = ctx.enter_context(nc.Block())

        TABLES = [(TABS[0:96, 0, :], rows["ada_b"]), (TABS[96:112, 0, :], rows["norm_mix_g"]),
                  (TABS[112:128, 0, :], rows["norm_ffn_g"])]
        at = 0
        for name, n in (("sconv", 12), ("conf_b1", 16), ("conf_dw_b", 8), ("conf_ln_g", 8),
                        ("conf_ln_b", 8), ("c", 8)):
            TABLES.append((TABS[at:at + n, 1, :], rows[name]))
            at += n
        TABLES += [(TABS[:, 2, :], rows["dw"][0:P]), (TABS[0:NDW - P, 3, :], rows["dw"][P:NDW])]

        @block.sync
        def _(sp):
            for dst, src in TABLES:
                sp.dma_start(dst, src).then_inc(tabs_in, 16)
            for at, (kind, n) in enumerate(ITEMS):
                if at >= NSLOT:
                    wait_used(sp, at - NSLOT)
                src = W0[n] if kind == "w" else cols(i["ada_w"][n // 24], (n % 24) * QW)
                sp.dma_start(slot(at), src).then_inc(ring[at % NSLOT], 16)

            def expert(l, e, b):
                g = i["moe_w_gate"][l].rearrange("e (k p) f -> e p k f", p=P)
                u = i["moe_w_up"][l].rearrange("e (k p) f -> e p k f", p=P)
                dw = i["moe_w_down"][l].rearrange("e (k p) n -> e p k n", p=P)
                at = b * EXP
                wgu = W[:, at:at + 2 * KC * FE].rearrange("p (k n) -> p k n", k=KC)
                wd = W[:, at + 2 * KC * FE:at + EXP].rearrange("p (k n) -> p k n", k=2)
                s = e_in[l][b]

                def pick(w):
                    return w[e] if isinstance(e, int) else w[bass.ds(e, 1)].rearrange("e p k n -> (e p) k n")
                sp.dma_start(wgu[:, :, 0:FE], pick(g)).then_inc(s, 16)
                sp.dma_start(wgu[:, :, FE:2 * FE], pick(u)).then_inc(s, 16)
                sp.dma_start(wd, pick(dw)).then_inc(s, 16)

            def experts(l):
                for e in range(NEB):
                    expert(l, e, e)
                sp.wait_ge(tab_ok, l + 1)

                def after(e3):
                    done = sp.value_load(RT[0:1, bass.ds(e3 + 1, 1)], min_val=1, max_val=MAXT)
                    sp.wait_ge(dn[l], done)
                with sp.Fori(1, NE // NEB) as j:
                    for b in range(NEB):
                        after(j * NEB + (b - NEB))
                        expert(l, j * NEB + b, b)
                last = NE - 1
                after(last - NEB)
                expert(l, last, last % NEB)
                return sp.value_load(RT[0:1, 0:1], min_val=1, max_val=MOST)

            sp.wait_ge(full, USED0[-1])
            sp.wait_ge(ada_fin, NADA)
            for b in range(NBROW):
                sp.wait_ge(brow_out[b], 16 * 4)
            sp.wait_ge(zeroed, 16 * NH)
            nt = experts(0)
            sp.wait_ge(dn[0], nt)
            for n in range(NW1):
                if n == 2:
                    sp.wait_ge(c_in[0][NB - 1][1], 16)
                if n >= NSLOT1:
                    sp.wait_ge(full, USED1[n - NSLOT1])
                sp.dma_start(slot(n, NSLOT1), W1[n]).then_inc(ring[n % NSLOT1], 16)
            sp.wait_ge(full, USED1[-1])
            sp.wait_ge(free["D"], emptied(GROUPS["var"] - 1))
            experts(1)
            for b in range(NB):
                sp.wait_ge(out_ok, b + 1)
                sp.dma_start(out_rows[:, b, :], OUTS[b]).then_inc(o_out, 16)
            sp.wait_ge(o_out, 16 * NB)

        @block.gpsimd
        def _(pool):
            pool.memset(IDENT[:], 0.0).then_inc(const, 1)
            pool.memset(ONES[:], 1.0).then_inc(const, 1)
            pool.memset(EPSC[:], EPS).then_inc(const, 1)
            pool.wait_ge(const, 3)
            pool.affine_select(out=IDENT[:], in_=IDENT[:], compare_op=ALU.not_equal, fill=1.0,
                               base=0, pattern=[[-1, P]], channel_multiplier=1).then_inc(const, 1)
            pool.affine_select(out=TRI[:], in_=ONES[:], compare_op=ALU.is_gt, fill=0.0,
                               base=0, pattern=[[1, P]], channel_multiplier=-1).then_inc(const, 1)
            pool.iota(IOTA[:], pattern=[[1, P]], base=0, channel_multiplier=0,
                      allow_small_or_imprecise_dtypes=True).then_inc(const, 1)
            pool.iota(TOKF[:], pattern=[[P, NB]], base=0, channel_multiplier=1,
                      allow_small_or_imprecise_dtypes=True).then_inc(const, 1)
            pool.memset(PSCR[:], 0.0).then_inc(const, 1)
            pool.memset(ZERO, 0.0).then_inc(const, 1)
            pool.wait_ge(sgu_in, 64)
            pool.affine_select(out=SGW, in_=SGW, compare_op=ALU.is_ge, fill=0.0, base=0,
                               pattern=[[0, HEADS], [-1, P]], channel_multiplier=1).then_inc(sgw_ok, 1)

            pool.wait_ge(const, 9)
            rest = y_dram[LEAST * P:MOST * P, :].rearrange("(t p) d -> p t d", p=P)
            zeros = ZERO.unsqueeze(1).broadcast_to([P, MOST - LEAST, HT])
            for q in range(16):
                if q == 4:
                    for h in range(NH):
                        pool.dma_start(rest[:, :, HT * h:HT * h + HT], zeros).then_inc(zeroed, 16)
                l, s = q // 8, (2, 5)[q // 4 % 2]
                n = 24 * l + 4 * s + q % 4
                pool.wait_ge(ada_fin, n + 1)
                pool.dma_start(g_dram[q // 4:q // 4 + 1, q % 4 * QW:(q % 4 + 1) * QW], BROW[q % NBROW]
                               ).then_inc(brow_out[q % NBROW], 16)

            for l in range(NL):
                for b in range(NB):
                    pool.wait_ge(xn_ok, 8 * (2 * l + 1) + b + 1)
                    pool.dma_start(xn_dram[P * b:P * b + P, :], XN[b // 4][:, b % 4, :]).then_inc(xn_out[l], 16)
                pool.wait_ge(tab_ok, l + 1)
                pool.wait_ge(xn_out[l], 16 * NB)
                nt = pool.value_load(RT[0:1, 0:1], min_val=1, max_val=MOST)

                def gather():
                    return pool.indirect_dma_start(
                        out=XG, out_offset=None, in_=xn_dram,
                        in_offset=bass.IndirectOffsetOnAxis(ap=TCUR[:, 0:1], axis=0)).then_inc(xg_in[l], 16)
                pool.tensor_tensor(PSCR[:, l:l + 1], PSCR[:, 2:3], PSCR[:, 2:3], ALU.add).then_inc(held[l], 1)
                pool.tensor_copy(TCUR[:], TOKI[:, 0:1]).then_inc(cur_ok[l], 1)
                pool.wait_ge(cur_ok[l], 1)
                gather()
                with pool.Fori(0, nt) as t:
                    pool.wait_ge(xg_in[l], t * 16 + 16)
                    pool.tensor_copy(TCUR[:], TOKI[:, bass.ds(t + 1, 1)]).then_inc(cur_ok[l], 1)
                    pool.wait_ge(cur_ok[l], t + 2)
                    pool.wait_ge(xtr[l], t + 1)
                    pool.wait_ge(held[l], t + 1)
                    pool.tensor_tensor(PSCR[:, l:l + 1], PSCR[:, 2:3], PSCR[:, 2:3], ALU.add).then_inc(held[l], 1)
                    gather()
                pool.wait_ge(zeroed, 16 * NH)
                pool.wait_ge(y_out[l], nt * 16 + 16)
                pool.wait_ge(xg_in[l], nt * 16 + 16)
                pool.wait_ge(held[l], nt + 1)
                pool.tensor_tensor(PSCR[:, l:l + 1], PSCR[:, 2:3], PSCR[:, 2:3], ALU.add).then_inc(held[l], 1)
                for b in range(NB):
                    if b == NY:
                        pool.wait_ge(xup, 16 * l + 8 + NY0 + 1)
                    for s, dst in ((0, Y1), (1, Y2)):
                        pool.indirect_dma_start(
                            out=dst[y_of(b)], out_offset=None, in_=y_dram,
                            in_offset=bass.IndirectOffsetOnAxis(ap=SLOTU[:, s, b:b + 1], axis=0)
                        ).then_inc(c_in[l][b][s], 16)

        @block.scalar
        def _(act):
            for n in range(2):
                act.dma_start(X[:, 4 * n:4 * n + 4, :], x_rows[:, 4 * n:4 * n + 4, :]).then_inc(xl[n], 16)
            act.dma_start(SGW, i["sgu_w"][0].rearrange("h t s -> t h s")).then_inc(sgu_in, 16)
            act.dma_start(LNG, on_all(i["sgu_ln_g"][0], DA)).then_inc(sgu_in, 16)
            act.dma_start(LNB, on_all(i["sgu_ln_b"][0], DA)).then_inc(sgu_in, 16)
            act.dma_start(SBB.rearrange("p a b -> p (a b)"),
                          on_all(i["sgu_b"][0].rearrange("h t -> (h t)"), HEADS * P)).then_inc(sgu_in, 16)
            act.dma_start(RW[:], i["router_w"].rearrange("(k p) e -> p k e", p=P)).then_inc(small_in, 16)
            act.dma_start(RB[:], on_all(i["router_bias"], NE)).then_inc(small_in, 16)
            act.wait_ge(pt_ok, 2)
            act.activation(CA[:], PT[:, COL_C:COL_C + KC], ACT.Silu).then_inc(ca_ok, 1)

            steps = [0]

            def link(ins):
                steps[0] += 1
                ins.then_inc(act_ch, 1)
                act.wait_ge(act_ch, steps[0])

            def gate_rows(dst, n):
                for b in range(NBROW):
                    act.wait_ge(brow_out[b], 16 * (n + 1))
                act.dma_start(dst, on_all(g_dram[n], D)).then_inc(gb_in[n], 16)

            def rms_sums(r, h):
                if r == 0:
                    act.wait_ge(xl[h], 16)
                for b in range(4 * h, 4 * h + 4):
                    if r:
                        act.wait_ge(xup, 8 * (r - 1) + b + 1)
                    link(act.activation(JUNK, X[:, b, :], ACT.Square, accum_out=SS[:, b:b + 1]))
                s = slice(4 * h, 4 * h + 4)
                act.activation(SD[:, s], SS[:, s], ACT.Sqrt, bias=EPSC[:], scale=1.0 / D).then_inc(rms_sd, 1)

            def evict_ht(r, l, ffn, h):
                for k in range(0, KC, 2):
                    act.wait_ge(tr, 16 * r + 8 * h + k + 1)
                    act.wait_ge(ada_fin, NADA0 if r == 0 else NADA)
                    act.activation(HTR[:, k, HT * h:HT * h + HT], TB_[0][:], ACT.Identity,
                                   bias=MC[:, l, 2 * ffn + 1, k:k + 1],
                                   scale=MC[:, l, 2 * ffn, k:k + 1]).then_inc(tev_a, 1)

            def take(g):
                act.wait_ge(full, g + 1)
                return M[g % 4]

            def experts(l):
                act.wait_ge(tab_ok, l + 1)
                nt = act.value_load(RT[0:1, 0:1], min_val=1, max_val=MOST)
                gate_rows(GBF, 2 * l + 1)
                if l == NL - 1:
                    act.dma_start(FGB, on_all(i["final_norm_g"], D)).then_inc(small_in, 16)

                def evict_tile(n_tr):
                    act.wait_ge(xtr[l], n_tr)
                    for k in range(4):
                        ins = act.activation(XT[:, k, :], TB_[0][:, k * P:(k + 1) * P], ACT.Identity,
                                             bias=MC[:, l, 3, k:k + 1], scale=MC[:, l, 2, k:k + 1])
                    ins.then_inc(xt_a[l], 1)
                evict_tile(1)
                act.sem_inc(y_out[l], 16)

                def hidden(t):
                    act.wait_ge(gu[l], t + 1)
                    act.activation(SG, M[0][:, 0:FE], ACT.Silu).then_inc(sg_ok[l], 1)
                    evict_tile(t + 2)

                def store(t):
                    act.wait_ge(ys_d[l], t + 2)
                    act.dma_start(y_dram[bass.ds(t * P, P), :], YS).then_inc(y_out[l], 16)
                hidden(0)
                with act.Fori(1, nt) as t:
                    hidden(t)
                    store(t - 1)
                store(nt - 1)

            def scores(l):
                act.wait_ge(lg, 2 * l + 1)
                act.activation(SCT[:, 0:HT], X0[0:NE, :], ACT.Sigmoid).then_inc(sct_ok, 1)
                act.wait_ge(lg, 2 * l + 2)
                act.activation(SCT[:, HT:T], M[0][0:NE, :], ACT.Sigmoid).then_inc(sct_ok, 1)
                act.wait_ge(sct_tr, l + 1)
                act.activation(SCO.rearrange("p a b -> p (a b)"), X1[:, 0:ne], ACT.Copy).then_inc(sco_ok, 1)

            rms_sums(0, 0)
            rms_sums(0, 1)
            evict_ht(0, 0, 0, 0)
            evict_ht(0, 0, 0, 1)
            for n in range(8):
                c, b = QW * (n // 4), 2 * (n % 4)
                act.activation(V[:, b:b + 2, c:c + QW],
                               take(GROUPS["v"] + n)[:].rearrange("p (b c) -> p b c", b=2),
                               ACT.Gelu).then_inc(free["A"], 1)
            act.wait_ge(ln_var, 1)
            act.activation(SD[:], MV[:, :, 1], ACT.Sqrt, bias=EPSC[:]).then_inc(ln_sd, 1)
            for n in range(8):
                act.activation(PB[:, n // 2, HT * (n % 2):HT * (n % 2) + HT],
                               take(GROUPS["cg"] + n)[:], ACT.Copy).then_inc(free["A"], 1)
            act.wait_ge(full, GROUPS["sgu"] + 8)
            act.wait_ge(free["D"], emptied(GROUPS["bg"]))
            gate_rows(GB0, 0)
            for n in range(8):
                if n >= 2:
                    act.wait_ge(ya_ok, n - 1)
                act.activation(GU[n % 2], take(GROUPS["u"] + n)[:], ACT.Gelu).then_inc(free["A"], 1)
            for h in range(NH):
                rms_sums(1, h)
                evict_ht(1, 0, 1, h)
            scores(0)
            experts(0)
            for h in range(NH):
                rms_sums(2, h)
            for h in range(NH):
                evict_ht(2, 1, 0, h)
            for n in range(16):
                g = GROUPS["w1"] + 2 * n
                ct, h = w1_group(n)
                if h == 0:
                    if ct >= 2:
                        act.wait_ge(cv_ps, ct - 1)
                    for j in range(PTAPS[ct]):
                        c0 = COL_DW + KC * (CTAPS - 2 - j) + ct
                        ins = act.activation(DIAG[ct % 2][:, j, :], IDENT[:], ACT.Copy, scale=PT[:, c0:c0 + 1])
                    ins.then_inc(diag_ok, 1)
                if n >= 2:
                    act.wait_ge(free["D"], emptied(g - 3))
                act.activation(SIG[n % 2], take(g)[:], ACT.Sigmoid,
                               bias=PT[:, COL_B1 + KC + ct:COL_B1 + KC + ct + 1]).then_inc(free["A"], 1)
            act.wait_ge(conv_ok, KC)
            gate_rows(GB1, 2)
            act.dma_start(B2B, on_all(i["conf_b2"][0], D)).then_inc(gb_in[2], 16)
            for h in range(NH):
                s = slice(HT * h, HT * h + HT)
                for k in range(KC):
                    act.wait_ge(cen_ok, KC * h + k + 1)
                    m = KC * h + k - 2
                    if m >= 0 and m % KC < KC - 1:
                        act.wait_ge(sq1_used, (KC - 1) * (m // KC) + m % KC + 1)
                    elif m >= 0:
                        act.wait_ge(full, GROUPS["var"] + m // KC + 1)
                    act.activation(SQ[k % 2], CV[:, k, s], ACT.Square).then_inc(sq1_ok, 1)
                act.activation(RSB[h], take(GROUPS["var"] + h)[:], ACT.Sqrt, bias=EPSC[:],
                               scale=1.0 / D).then_inc(free["A"], 1)
            for h in range(NH):
                s = slice(HT * h, HT * h + HT)
                for k in range(KC):
                    act.wait_ge(nrm_ok, KC * h + k + 1)
                    act.activation(CV[:, k, s], CV[:, k, s], ACT.Silu,
                                   bias=PT[:, COL_LNB + k:COL_LNB + k + 1],
                                   scale=PT[:, COL_LNG + k:COL_LNG + k + 1]).then_inc(z_ok, 1)
            for h in range(NH):
                rms_sums(3, h)
                evict_ht(3, 1, 1, h)
            scores(1)
            experts(1)
            rms_sums(4, 0)
            rms_sums(4, 1)

        @block.tensor
        def _(pe):
            pe.wait_ge(const, 7)
            pe.wait_ge(tabs_in, 16 * 11)
            for n, m in enumerate((P, NTAB_B, P, NDW - P)):
                ins = pe.transpose(X0[:, 128 * n:128 * n + m], TABS[0:m, n, :], IDENT[0:m, 0:m])
            ins.then_inc(pt_ps, 1)
            pe.wait_ge(sgw_ok, 1)
            for h in range(HEADS):
                ins = pe.transpose(X1[:, P * h:P * h + P], SGW[:, h, :], IDENT[:])
            ins.then_inc(sgt_ps, 1)

            def reduce_ada(n):
                pe.wait_ge(ada_used, n + 1)
                if n == 0:
                    pe.wait_ge(pt_ok, 4)
                elif n == 1:
                    pe.wait_ge(sgt_ok, 1)
                else:
                    pe.wait_ge(ada_fin, n - 1)
                dst = (X0, X1)[n % 2]
                l, s = n // 24, (n % 24) // 4
                if s in (2, 5):
                    for c in range(2):
                        o = dst[0:1, P * c:P * c + P]
                        col = COL_ADAB + 48 * l + 8 * s + 2 * (n % 4) + c
                        pe.matmul(o, ONES[:, 0:1], ACC[n % 2][:, P * c:P * c + P], start=True, stop=False)
                        ins = pe.matmul(o, PT[:, col:col + 1], IDENT[:], start=False, stop=True)
                else:
                    for c in range(2):
                        ins = pe.matmul(dst[:, c:c + 1], ACC[n % 2][:, P * c:P * c + P], ONES[:, 0:1],
                                        start=True, stop=True)
                ins.then_inc(red, 1)

            def transposes(r, h, behind=None):
                for k in range(KC):
                    q = 16 * r + 8 * h + k
                    if k == 0:
                        pe.wait_ge(xn_ok, 8 * r + 4 * h + 4)
                    if q >= 2:
                        pe.wait_ge((tev_a, tev_d)[q % 2], q // 2)
                    for b in range(4):
                        ins = pe.transpose(TB_[q % 2][:, P * b:P * b + P],
                                           XN[h][:, b, P * k:P * k + P], IDENT[:])
                    ins.then_inc(tr, 1)
                    if behind is not None and k >= 2:
                        behind(k - 2)
                if behind is not None:
                    behind(KC - 2)
                    behind(KC - 1)

            def ht_ready(r, h):
                pe.wait_ge(tev_a, 8 * r + 4 * h + 4)
                pe.wait_ge(tev_d, 8 * r + 4 * h + 4)

            def main(g):
                if g >= 4:
                    pe.wait_ge(free[CONSUMER[g - 4]], emptied(g - 4))
                return M[g % 4]

            def product(g, lhs, rhs, kc=KC):
                dst = main(g)
                for k in range(kc):
                    ins = pe.matmul(dst[:], lhs(k), rhs(k), start=(k == 0), stop=(k == kc - 1))
                return ins.then_inc(full, 1)

            def cols_of(g, w, n):
                c, h = n // 2, n % 2
                return product(g, lambda k: w[:, k, P * c:P * c + P],
                               lambda k: HTR[:, k, HT * h:HT * h + HT])

            def logits_first(r):
                ht_ready(r, 0)
                pe.wait_ge(ada_fin, NADA)
                pe.wait_ge(small_in, 32)
                for k in range(KC):
                    ins = pe.matmul(X0[0:NE, :], RW[:, k, :], HTR[:, k, 0:HT], start=(k == 0),
                                    stop=(k == KC - 1))
                ins.then_inc(lg, 1)

            def logits_second(r, k, g):
                q = 16 * r + 8 + k
                pe.wait_ge((tev_a, tev_d)[q % 2], q // 2 + 1)
                if k == 0:
                    pe.wait_ge(free["A"], CONSUMER[:g + 1].count("A"))
                    pe.wait_ge(free["D"], CONSUMER[:g + 1].count("D"))
                ins = pe.matmul(M[0][0:NE, :], RW[:, k, :], HTR[:, k, HT:T], start=(k == 0),
                                stop=(k == KC - 1))
                if k == KC - 1:
                    ins.then_inc(lg, 1)

            def project(g0, src, item, r, ready, beside=lambda p, j: None):
                for p in range(4):
                    ready(p)
                    for j in range(4):
                        rows_of(g0 + 4 * p + j, src, item(j), p)
                        if beside(p, j) is not None:
                            reduce_ada(beside(p, j))
                    if p == 2:
                        transposes(r, 0)
                logits_first(r)
                transposes(r, 1, lambda k: logits_second(r, k, g0 + 15))

            def rows_of(g, src, w, n):
                dst = main(g)
                for b in range(2):
                    t0 = P * (2 * n + b)
                    for k in range(KC):
                        ins = pe.matmul(dst[:, QW * b:QW * b + QW], src[:, k, t0:t0 + P], w[:, k, :],
                                        start=(k == 0), stop=(k == KC - 1))
                return ins.then_inc(full, 1)

            def item0(wn, g0, of):
                at = item_at("w", wn)
                wait_item(pe, at)
                w = slot(at)
                for n in range(4):
                    of(g0 + n, w, n)
                    for a in beside_of(wn, n):
                        reduce_ada(a)

            def experts(l, r):
                pe.wait_ge(sct_ok, 2 * l + 2)
                for n in range(NB):
                    ins = pe.transpose(X1[:, NE * n:NE * n + NE], SCT[:, P * n:P * n + P], IDENT[0:NE, 0:NE])
                ins.then_inc(sct_tr, 1)
                pe.wait_ge(mm_ok, l + 1)
                mm = MM.rearrange("p a b -> p (a b)")
                pe.matmul(X1[:, 0:ne], TRI[:], mm, start=True, stop=True)
                pe.matmul(X1[:, ne:2 * ne], ONES[:], mm, start=True, stop=True).then_inc(cnt, 1)
                pe.wait_ge(oh_ok, l + 1)
                for n in range(2 * NB):
                    ins = pe.matmul(X0[:, 0:2 * MAXT], RO[:, n, :],
                                    QQ[:, n].rearrange("p a b -> p (a b)"), start=(n == 0),
                                    stop=(n == 2 * NB - 1))
                ins.then_inc(tok_ps, 1)
                pe.wait_ge(tab_ok, l + 1)
                nt = pe.value_load(RT[0:1, 0:1], min_val=1, max_val=MOST)
                def transpose_tile(n_in):
                    pe.wait_ge(xg_in[l], n_in)
                    for k in range(KC):
                        ins = pe.transpose(TB_[k // 4][:, P * (k % 4):P * (k % 4) + P],
                                           XG[:, P * k:P * k + P], IDENT[:])
                    ins.then_inc(xtr[l], 1)
                def gate_up(t, at, thr):
                    pe.wait_ge(xt_a[l], t + 1)
                    pe.wait_ge(xt_d[l], t + 1)
                    for b in range(NEB):
                        pe.wait_ge(e_in[l][b], thr[b])
                    for k in range(KC):
                        ins = pe.matmul(M[0][:], XT[:, k, :], W[:, bass.ds(at + k * 2 * FE, 2 * FE)],
                                        start=(k == 0), stop=(k == KC - 1))
                    ins.then_inc(gu[l], 1)

                def transpose_hidden(t):
                    pe.wait_ge(ag_ok[l], t + 1)
                    for k in range(2):
                        ins = pe.transpose(X0[:, P * k:P * k + P], AG[:, P * k:P * k + P], IDENT[:])
                    ins.then_inc(atr[l], 1)

                def down(t, at):
                    pe.wait_ge(at_ok[l], t + 1)
                    pe.wait_ge(ys_d[l], t + 1)
                    for h in range(NH):
                        for k in range(2):
                            ins = pe.matmul(M[1 + h][:], AT[:, k, :],
                                            W[:, bass.ds(at + 2 * KC * FE + k * D + h * HT, HT)],
                                            start=(k == 0), stop=(k == 1))
                    ins.then_inc(dn[l], 1)

                def expert_at(t):
                    return pe.value_load(RT[0:1, bass.ds(t + MAXT * 4, 1)], min_val=0,
                                         max_val=(NEB - 1) * EXP)

                transpose_tile(16)
                gate_up(0, 0, [48, 0, 0])
                transpose_tile(32)
                transpose_hidden(0)
                with pe.Fori(1, nt) as t:
                    thr = [pe.value_load(RT[0:1, bass.ds(t + MAXT * (1 + b), 1)], min_val=0, max_val=48 * NE)
                           for b in range(NEB)]
                    gate_up(t, expert_at(t), thr)
                    transpose_tile(t * 16 + 32)
                    down(t - 1, expert_at(t - 1))
                    transpose_hidden(t)
                down(nt - 1, expert_at(nt - 1))
                pe.wait_ge(ys_d[l], nt + 1)
                pe.wait_ge(xt_a[l], nt + 1)
                pe.wait_ge(xt_d[l], nt + 1)

            for n in range(NADA0):
                reduce_ada(n)
            transposes(0, 0)
            transposes(0, 1)

            def v_of(g, w, n):
                ht_ready(0, n // 2)
                rows_of(g, HTR, w, n)
            for j in range(2):
                item0(WV + j, GROUPS["v"] + 4 * j, v_of)
            for j in range(2):
                item0(WCG + j, GROUPS["cg"] + 4 * j, cols_of)
            pe.wait_ge(sgt_ok, 1)
            for n in range(8):
                hd, h = n // 2, n % 2
                dst = main(GROUPS["sgu"] + n)
                for c in range(4):
                    b = 4 * h + c
                    pe.wait_ge(v_ok, b + 1)
                    ins = pe.matmul(dst[:, P * c:P * c + P], V[:, b, P * hd:P * hd + P],
                                    SGT[:, hd, :], start=True, stop=True)
                ins.then_inc(full, 1)
            for name, wn in (("hb", WHB), ("bg", WBG), ("u", WU)):
                for j in range(2):
                    item0(wn + j, GROUPS[name] + 4 * j, cols_of)
            pe.wait_ge(ya_ok, 8)
            pe.wait_ge(free["D"], emptied(GROUPS["bg"] + 7))
            def wo_item(j):
                at = item_at("w", WWO + j)
                wait_item(pe, at)
                return slot(at)
            project(GROUPS["wo"], YC, wo_item, 1, lambda p: None, beside_out)
            experts(0, 1)
            transposes(2, 0)
            transposes(2, 1)
            def item1(n):
                before = len(range(n % NSLOT1, ITEM0, NSLOT))
                pe.wait_ge(ring[n % NSLOT1], 16 * (before + n // NSLOT1 + 1))
                return slot(n, NSLOT1)

            def conv_taps(c):
                pe.wait_ge(diag_ok, c + 1)
                g = [GROUPS["w1"] + 2 * n + 1 for n in range(16) if w1_group(n)[0] == c][-1]
                pe.wait_ge(free["D"], emptied(g))
                if c >= 1:
                    pe.wait_ge(conv_ok, c)
                for h in range(NH):
                    for j in range(PTAPS[c]):
                        d = j + 1
                        lo = d if h == 0 else 0
                        ins = pe.matmul((X0, X1)[h][:, lo:HT], DIAG[c % 2][:, j, :],
                                        GT[:, c, HT * h + lo - d:HT * h + HT - d],
                                        start=(j == 0), stop=(j == PTAPS[c] - 1))
                ins.then_inc(cv_ps, 1)

            def mean(c):
                pe.wait_ge(conv_ok, c + 1)
                if c == 0:
                    pe.wait_ge(tev_a, 8 * 3)
                    pe.wait_ge(tev_d, 8 * 3)
                for h in range(NH):
                    ins = pe.matmul(TB_[h][:], ONES[:], CV[:, c, HT * h:HT * h + HT],
                                    start=(c == 0), stop=(c == KC - 1), skip_group_check=True)
                return ins
            for n in range(16):
                c, h = w1_group(n)
                ht_ready(2, h)
                for part in range(2):
                    w = item1(2 * (c // 2) + part)
                    cols_of(GROUPS["w1"] + 2 * n + part, w, 2 * (c % 2) + h)
                if n >= 3 and n % 2:
                    m = n // 2 - 1
                    conv_taps(m)
                    if m:
                        mean(m - 1)
            conv_taps(KC - 1)
            mean(KC - 2)
            mean(KC - 1).then_inc(mu_ps, 1)
            for h in range(NH):
                dst = main(GROUPS["var"] + h)
                for k in range(KC):
                    pe.wait_ge(sq1_ok, KC * h + k + 1)
                    ins = pe.matmul(dst[:], ONES[:], SQ[k % 2], start=(k == 0), stop=(k == KC - 1))
                    ins.then_inc(*((sq1_used, 1) if k < KC - 1 else (full, 1)))
            project(GROUPS["w2"], CV, lambda j: item1(8 + j), 3,
                    lambda p: pe.wait_ge(z_ok, KC * (p // 2) + KC))
            experts(1, 3)

        @block.vector
        def _(dve):
            steps = [0]

            def link(ins):
                steps[0] += 1
                ins.then_inc(dch, 1)
                dve.wait_ge(dch, steps[0])

            def tt(o, a, b, op):
                return dve.tensor_tensor(o, a, b, op)

            for n, m in enumerate((P, NTAB_B, P, NDW - P)):
                dve.wait_ge(pt_ps, 1)
                c0 = (0, P, COL_DW, COL_DW + P)[n]
                dve.tensor_copy(PT[:, c0:c0 + m], X0[:, 128 * n:128 * n + m]).then_inc(pt_ok, 1)
            dve.wait_ge(sgt_ps, 1)
            dve.tensor_copy(SGT.rearrange("p a b -> p (a b)"), X1[:]).then_inc(sgt_ok, 1)

            def ada(n):
                at = item_at("a", n)
                wait_item(dve, at)
                if n == 0:
                    dve.wait_ge(ca_ok, 1)
                    dve.wait_ge(pt_ok, 4)
                if n >= 2:
                    dve.wait_ge(red, n - 1)
                acc, w = ACC[n % 2], slot(at)
                link(dve.tensor_scalar(acc, w[:, 0, :], CA[:, 0:1], None, ALU.mult))
                for k in range(1, KC):
                    ins = dve.scalar_tensor_tensor(out=acc, in0=w[:, k, :], scalar=CA[:, k:k + 1],
                                                   in1=acc, op0=ALU.mult, op1=ALU.add)
                    if k < KC - 1:
                        link(ins)
                ins.then_inc(ada_used, 1)

            def ada_finish(n):
                l, s, h = n // 24, (n % 24) // 4, n % 4
                dve.wait_ge(red, n + 1)
                src = (X0, X1)[n % 2]
                if s in (2, 5):
                    q = (2 * l + s // 3) * 4 + h
                    if q >= NBROW:
                        dve.wait_ge(brow_out[q % NBROW], 16 * (q // NBROW))
                    dve.tensor_copy(BROW[q % NBROW], src[0:1, 0:QW]).then_inc(ada_fin, 1)
                    return
                o = MC[:, l, 2 * (s // 3) + (1 - s % 3), 2 * h:2 * h + 2]
                c0 = COL_ADAB + 48 * l + 8 * s + 2 * h
                if s % 3 == 0:
                    tt(o, src[:, 0:2], PT[:, c0:c0 + 2], ALU.add).then_inc(ada_fin, 1)
                else:
                    link(tt(o, src[:, 0:2], PT[:, c0:c0 + 2], ALU.add))
                    g0 = (COL_NMIX if s == 1 else COL_NFFN) + 8 * l + 2 * h
                    dve.scalar_tensor_tensor(out=o, in0=o, scalar=1.0, in1=PT[:, g0:g0 + 2],
                                             op0=ALU.add, op1=ALU.mult).then_inc(ada_fin, 1)

            def beside(wn, n, evict=None):
                todo = beside_of(wn, n)
                for a in todo:
                    ada(a)
                if evict is not None:
                    evict()
                for a in todo:
                    ada_finish(a)

            def rms_apply(r, h):
                dve.wait_ge(rms_sd, 2 * r + h + 1)
                s = slice(4 * h, 4 * h + 4)
                link(dve.reciprocal(RSTD[:, s], SD[:, s]))
                for b in range(4 * h, 4 * h + 4):
                    if r < 4:
                        dve.tensor_scalar(XN[h][:, b % 4, :], X[:, b, :], RSTD[:, b:b + 1], None,
                                          ALU.mult).then_inc(xn_ok, 1)
                        continue
                    dve.wait_ge(small_in, 48)
                    dve.scalar_tensor_tensor(out=OUTS[b], in0=X[:, b, :], scalar=RSTD[:, b:b + 1],
                                             in1=FGB, op0=ALU.mult, op1=ALU.mult).then_inc(out_ok, 1)

            def evict_ht(r, l, ffn, h):
                dve.wait_ge(ada_fin, NADA if r else NADA0)
                for k in range(1, KC, 2):
                    dve.wait_ge(tr, 16 * r + 8 * h + k + 1)
                    dve.tensor_scalar(HTR[:, k, HT * h:HT * h + HT], TB_[1][:],
                                      MC[:, l, 2 * ffn, k:k + 1], MC[:, l, 2 * ffn + 1, k:k + 1],
                                      ALU.mult, ALU.add).then_inc(tev_d, 1)

            def take(g):
                dve.wait_ge(full, g + 1)
                return M[g % 4]

            def first_max(o_oh, src, tmp, red1, pri):
                shape = list(src.shape)
                link(dve.tensor_reduce(red1, src, AX.X, ALU.max))
                link(tt(tmp, src, red1.unsqueeze(len(shape) - 1).broadcast_to(shape), ALU.is_equal))
                link(tt(tmp, tmp, pri, ALU.mult))
                link(dve.tensor_reduce(red1, tmp, AX.X, ALU.max))
                link(tt(o_oh, tmp, red1.unsqueeze(len(shape) - 1).broadcast_to(shape), ALU.is_equal))

            def route(l):
                full3 = [P, NB, NE]
                g4 = [P, NB * NG, EG]

                def grp(a):
                    return a.rearrange("p a b -> p (a b)").rearrange("p (g e) -> p g e", e=EG)
                link(dve.tensor_scalar(PRI, IOTA[:, 0:NE].unsqueeze(1).broadcast_to(full3), -1.0,
                                       float(NE), ALU.mult, ALU.add))
                dve.wait_ge(sco_ok, l + 1)
                link(tt(BIA, SCO, RB[:].unsqueeze(1).broadcast_to(full3), ALU.add))
                b4 = grp(BIA)
                pa = R[:, 3, 10 * ne:10 * ne + 6 * NB * NG].rearrange("p (g e) -> p g e", e=6)
                tt(pa[:, :, 0:3], b4[:, :, 0:3], b4[:, :, 1:4], ALU.add)
                tt(pa[:, :, 3:5], b4[:, :, 0:2], b4[:, :, 2:4], ALU.add)
                link(tt(pa[:, :, 5:6], b4[:, :, 0:1], b4[:, :, 3:4], ALU.add))
                gs = SM[:, 0:32]
                link(dve.tensor_reduce(gs, pa, AX.X, ALU.max))
                gs3 = gs.rearrange("p (b g) -> p b g", g=NG)
                sel = SM[:, 32:64].rearrange("p (b g) -> p b g", g=NG)
                tmp = SM[:, 64:96].rearrange("p (b g) -> p b g", g=NG)
                one = SM[:, 96:104]
                first_max(sel, gs3, tmp, one, PRI[:, :, 0:NG])
                selb = SM[:, 32:64].unsqueeze(2).broadcast_to(g4)
                link(tt(grp(TA), grp(BIA), selb, ALU.mult))
                link(dve.tensor_scalar(grp(TB), selb, -1.0, BIG, ALU.add, ALU.mult))
                link(tt(MSK, TA, TB, ALU.add))
                first_max(OH1, MSK, TA, one, PRI)
                link(dve.scalar_tensor_tensor(out=MSK, in0=OH1, scalar=-2.0 * BIG, in1=MSK,
                                              op0=ALU.mult, op1=ALU.add))
                first_max(OH2, MSK, TA, one, PRI)
                tt(MM, OH1, OH2, ALU.add).then_inc(mm_ok, 1)
                s1, s2, ssum = SM[:, 0:8], SM[:, 8:16], SM[:, 16:24]
                link(tt(TA, SCO, OH1, ALU.mult))
                link(dve.tensor_reduce(s1, TA, AX.X, ALU.add))
                link(tt(TB, SCO, OH2, ALU.mult))
                link(dve.tensor_reduce(s2, TB, AX.X, ALU.add))
                link(tt(ssum, s1, s2, ALU.add))
                link(dve.reciprocal(ssum, ssum))
                tt(GATE[:, 0, :], s1, ssum, ALU.mult)
                link(tt(GATE[:, 1, :], s2, ssum, ALU.mult))
                dve.wait_ge(cnt, l + 1)
                link(dve.tensor_copy(TA.rearrange("p a b -> p (a b)"), X1[:, 0:ne]))
                base = SM[:, 32:48]
                link(dve.tensor_copy(base, X1[:, ne:ne + NE]))
                for b in range(1, NB):
                    link(tt(TA[:, b, :], TA[:, b, :], base, ALU.add))
                    link(tt(base, base, X1[:, ne + NE * b:ne + NE * b + NE], ALU.add))
                j7 = R[:, 3, 10 * ne:10 * ne + 7 * NE].rearrange("p (e j) -> p e j", j=7)
                link(dve.tensor_scalar(j7, IOTA[:, 1:8].unsqueeze(1).broadcast_to([P, NE, 7]),
                                       float(P), None, ALU.mult))
                link(tt(j7, base.unsqueeze(2).broadcast_to([P, NE, 7]), j7, ALU.is_gt))
                ntl, ca, cb = SM[:, 48:64], SM[:, 64:80], SM[:, 80:96]
                link(dve.tensor_reduce(ntl, j7, AX.X, ALU.add))
                link(dve.tensor_scalar(ntl, ntl, 1.0, None, ALU.add))
                link(dve.tensor_copy(ca, ntl))
                for s in (1, 2, 4, 8):
                    dve.tensor_copy(cb[:, 0:s], ca[:, 0:s])
                    link(tt(cb[:, s:NE], ca[:, s:NE], ca[:, 0:NE - s], ALU.add))
                    ca, cb = cb, ca
                inc = ca
                off = SM[:, 96:112]
                link(tt(off, inc, ntl, ALU.subtract))
                link(dve.tensor_scalar(off, off, float(P), None, ALU.mult))
                link(tt(TA, TA, off.unsqueeze(1).broadcast_to(full3), ALU.add))
                for s, oh in ((0, OH1), (1, OH2)):
                    link(tt(TB, TA, oh, ALU.mult))
                    link(dve.tensor_reduce(SLOTF[:, s, :], TB, AX.X, ALU.add))
                link(dve.tensor_copy(SLOTU[:], SLOTF[:]))
                si = SM[:, 0:16].bitcast(I32)
                sj = SM[:, 16:32].bitcast(I32)
                slf = SLOTF[:].rearrange("p a b -> p (a b)")
                link(dve.tensor_copy(si, slf))
                link(dve.tensor_scalar(sj, si, 7, None, ALU.arith_shift_right))
                qf, rf = SM[:, 32:48], SM[:, 112:128]
                link(dve.tensor_copy(qf, sj))
                link(dve.scalar_tensor_tensor(out=rf, in0=qf, scalar=-float(P), in1=slf,
                                              op0=ALU.mult, op1=ALU.add))
                q3 = [P, 16, MAXT]
                link(tt(QO, IOTA[:, 0:MAXT].unsqueeze(1).broadcast_to(q3),
                        qf.unsqueeze(2).broadcast_to(q3), ALU.is_equal))
                q4 = QO.rearrange("p (s b) q -> p s b q", s=TOPK)
                for s in range(TOPK):
                    tt(QG.rearrange("p (s b) q -> p s b q", s=TOPK)[:, s], q4[:, s],
                       GATE[:, s, :].unsqueeze(2).broadcast_to([P, NB, MAXT]), ALU.mult).then_inc(dch, 1)
                    steps[0] += 1
                    dve.wait_ge(dch, steps[0])
                    tt(q4[:, s], q4[:, s], TOKF[:].unsqueeze(2).broadcast_to([P, NB, MAXT]), ALU.mult)
                tt(RO, IOTA[:].unsqueeze(1).broadcast_to([P, 16, P]),
                   rf.unsqueeze(2).broadcast_to([P, 16, P]), ALU.is_equal).then_inc(oh_ok, 1)
                rowt = R[0:1, 3, 0:MAXT * NE].rearrange("p (t e) -> p t e", e=NE)
                ex = ROWT[:, 0:MAXT]
                sh = [1, MAXT, NE]
                link(tt(rowt, inc[0:1].unsqueeze(1).broadcast_to(sh),
                        IOTA[0:1, 0:MAXT].unsqueeze(2).broadcast_to(sh), ALU.is_le))
                link(dve.tensor_reduce(ex, rowt, AX.X, ALU.add))
                dve.tensor_copy(RTF[:, 0:1], inc[0:1, NE - 1:NE])
                dve.tensor_copy(RTF[:, 1 + NE:MAXT], IOTA[0:1, 1 + NE:MAXT])
                link(dve.tensor_copy(RTF[:, 1:1 + NE], inc[0:1]))
                sh6 = [1, MAXT, 6]
                row6 = R[0:1, 3, 0:MAXT * 6].rearrange("p (t e) -> p t e", e=6)
                for b in range(NEB):
                    th = ROWT[:, MAXT:MAXT + 6]
                    link(dve.tensor_scalar(th, IOTA[0:1, 0:6], float(NEB), float(b), ALU.mult, ALU.add))
                    link(tt(row6, th.unsqueeze(1).broadcast_to(sh6), ex.unsqueeze(2).broadcast_to(sh6),
                            ALU.is_le))
                    link(dve.tensor_reduce(ROWT[:, (2 + b) * MAXT:(3 + b) * MAXT], row6, AX.X, ALU.add))
                    link(dve.tensor_scalar(RTF[:, (1 + b) * MAXT:(2 + b) * MAXT],
                                           ROWT[:, (2 + b) * MAXT:(3 + b) * MAXT], 48.0, None, ALU.mult))
                bf = ROWT[:, 5 * MAXT:6 * MAXT]
                link(dve.scalar_tensor_tensor(out=bf, in0=ROWT[:, 2 * MAXT:3 * MAXT],
                                              scalar=-float(NEB), in1=ex, op0=ALU.mult, op1=ALU.add))
                link(dve.tensor_scalar(RTF[:, 4 * MAXT:5 * MAXT], bf, float(NEB), float(EXP),
                                       ALU.add, ALU.mult))
                link(dve.tensor_copy(RT[:], RTF[:]))
                dve.wait_ge(tok_ps, l + 1)
                link(dve.tensor_copy(GSLOT[:], X0[:, MAXT:2 * MAXT]))
                dve.tensor_copy(TOKI[:], X0[:, 0:MAXT]).then_inc(tab_ok, 1)

            def experts(l):
                nt = dve.value_load(RT[0:1, 0:1], min_val=1, max_val=MOST)

                def evict_tile(n_tr):
                    dve.wait_ge(xtr[l], n_tr)
                    for k in range(4, KC):
                        ins = dve.tensor_scalar(XT[:, k, :], TB_[1][:, (k - 4) * P:(k - 3) * P],
                                                MC[:, l, 2, k:k + 1], MC[:, l, 3, k:k + 1],
                                                ALU.mult, ALU.add)
                    ins.then_inc(xt_d[l], 1)
                evict_tile(1)
                dve.sem_inc(ys_d[l], 1)
                dve.wait_ge(gb_in[2 * l + 1], 16)

                def hidden(t):
                    dve.wait_ge(gu[l], t + 1)
                    dve.wait_ge(sg_ok[l], t + 1)
                    tt(AG, M[0][:, FE:2 * FE], SG, ALU.mult).then_inc(ag_ok[l], 1)
                    evict_tile(t + 2)

                def turned(t):
                    dve.wait_ge(atr[l], t + 1)
                    dve.tensor_copy(AT.rearrange("p a b -> p (a b)"), X0[:, 0:FE]).then_inc(at_ok[l], 1)

                def tile_out(t):
                    dve.wait_ge(dn[l], t + 1)
                    dve.wait_ge(y_out[l], t * 16 + 16)
                    g = GSLOT[:, bass.ds(t, 1)]
                    dve.scalar_tensor_tensor(out=YS[:, 0:HT], in0=M[1][:], scalar=g, in1=GBF[:, 0:HT],
                                             op0=ALU.mult, op1=ALU.mult)
                    dve.scalar_tensor_tensor(out=YS[:, HT:D], in0=M[2][:], scalar=g, in1=GBF[:, HT:D],
                                             op0=ALU.mult, op1=ALU.mult).then_inc(ys_d[l], 1)
                hidden(0)
                turned(0)
                with dve.Fori(1, nt) as t:
                    hidden(t)
                    tile_out(t - 1)
                    turned(t)
                tile_out(nt - 1)

            def combine(l, b):
                for s, y in ((0, Y1), (1, Y2)):
                    dve.wait_ge(c_in[l][b][s], 16)
                    ins = tt(X[:, b, :], X[:, b, :], y[y_of(b)], ALU.add)
                    if s == 0:
                        link(ins)
                ins.then_inc(xup, 1)

            def project_in(g0, r, l, gb, tmp, b2=None, beside=lambda p, j: None):
                for p in range(4):
                    if p == 2:
                        rms_apply(r, 0)
                    for j in range(4):
                        if beside(p, j) is not None:
                            ada(beside(p, j))
                        add_out(g0 + 4 * p + j, p, j, gb, tmp, b2)
                        if beside(p, j) is not None:
                            ada_finish(beside(p, j))
                    if p == 2:
                        evict_ht(r, l, 1, 0)
                rms_apply(r, 1)
                evict_ht(r, l, 1, 1)

            def add_out(g, p, j, gb, tmp, b2=None):
                c, b, n = QW * j, 2 * p, j
                sh = [P, 2, QW]
                t = tmp[n % 2].rearrange("p (b c) -> p b c", b=2)
                ps = take(g)[:].rearrange("p (b c) -> p b c", b=2)
                gate = gb[:, c:c + QW].unsqueeze(1).broadcast_to(sh)
                bias = None if b2 is None else b2[:, c:c + QW].unsqueeze(1).broadcast_to(sh)
                if b2 is None:
                    tt(t, ps, gate, ALU.mult).then_inc(free["D"], 1)
                    dve.wait_ge(free["D"], emptied(g))
                else:
                    tt(t, ps, bias, ALU.add).then_inc(free["D"], 1)
                    dve.wait_ge(free["D"], emptied(g))
                    link(tt(t, t, gate, ALU.mult))
                x = X[:, b:b + 2, c:c + QW]
                ins = tt(x, x, t, ALU.add)
                if j == 3:
                    ins.then_inc(xup, 2)

            for n in range(NADA0):
                if n == NADA0 // 2:
                    rms_apply(0, 0)
                    rms_apply(0, 1)
                ada(n)
                ada_finish(n)
            evict_ht(0, 0, 0, 0)
            evict_ht(0, 0, 0, 1)
            for n in range(8):
                beside(WV + n // 4, n % 4)
            dve.wait_ge(sgu_in, 64)
            for b in range(NB):
                dve.wait_ge(free["A"], emptied(GROUPS["v"] + 4 + b // 2))
                link(dve.bn_stats(BST[:, b, :], V[:, b, :]))
                ins = dve.bn_aggr(MV[:, b, :], BST[:, b, :])
            ins.then_inc(ln_var, 1)
            dve.wait_ge(ln_var, 1)
            dve.wait_ge(ln_sd, 1)
            link(dve.reciprocal(RSTD[:], SD[:]))
            for b in range(NB):
                v = V[:, b, :]
                link(dve.tensor_scalar(v, v, MV[:, b, 0:1], RSTD[:, b:b + 1], ALU.subtract, ALU.mult))
                link(tt(v, v, LNG, ALU.mult))
                tt(v, v, LNB, ALU.add).then_inc(v_ok, 1)
            for n in range(8):
                beside(WCG + n // 4, n % 4)
            for n in range(8):
                hd, h = n // 2, n % 2
                o = YC[:, hd, HT * h:HT * h + HT].rearrange("p (c t) -> p c t", t=P)
                tt(o, take(GROUPS["sgu"] + n)[:].rearrange("p (c t) -> p c t", t=P),
                   SBB[:, hd, :].unsqueeze(1).broadcast_to([P, 4, P]), ALU.add).then_inc(free["D"], 1)
            dve.wait_ge(free["A"], emptied(GROUPS["cg"] + 7))
            for n in range(8):
                c, h = n // 2, n % 2
                g = GROUPS["hb"] + n
                s = slice(HT * h, HT * h + HT)
                beside(WHB + n // 4, n % 4,
                       lambda: tt(PB[:, c, s], PB[:, c, s], take(g)[:], ALU.mult).then_inc(free["D"], 1))
                if h == 0:
                    continue
                dve.wait_ge(free["D"], emptied(g))
                o, p = YC[:, 4 + c, :], PB[:, c, :]

                def tap(j):
                    return PT[:, COL_SC + 4 * j + c:COL_SC + 4 * j + c + 1]
                link(dve.tensor_scalar(o, p, tap(BTAPS - 1), None, ALU.mult))
                for j in range(BTAPS - 2, -1, -1):
                    d = BTAPS - 1 - j
                    link(dve.scalar_tensor_tensor(out=o[:, d:T], in0=p[:, 0:T - d], scalar=tap(j),
                                                  in1=o[:, d:T], op0=ALU.mult, op1=ALU.add))
            for n in range(8):
                c, h = n // 2, n % 2
                o = YC[:, 4 + c, HT * h:HT * h + HT]
                g = GROUPS["bg"] + n
                beside(WBG + n // 4, n % 4,
                       lambda: tt(o, o, take(g)[:], ALU.mult).then_inc(free["D"], 1))
            for n in range(8):
                c, h = n // 2, n % 2
                o = YC[:, c, HT * h:HT * h + HT]

                def gate():
                    dve.wait_ge(free["A"], emptied(GROUPS["u"] + n))
                    tt(o, o, GU[n % 2], ALU.mult).then_inc(ya_ok, 1)
                beside(WU + n // 4, n % 4, gate)
            dve.wait_ge(gb_in[0], 16)
            project_in(GROUPS["wo"], 1, 0, GB0, TMPO, beside=beside_out)
            route(0)
            experts(0)
            for b in range(NB):
                if b == 5:
                    rms_apply(2, 0)
                combine(0, b)
            evict_ht(2, 1, 0, 0)
            rms_apply(2, 1)
            evict_ht(2, 1, 0, 1)
            for n in range(16):
                c, h = w1_group(n)
                g = GROUPS["w1"] + 2 * n + 1
                dve.wait_ge(free["A"], emptied(g - 1))
                dve.scalar_tensor_tensor(out=GT[:, c, HT * h:HT * h + HT], in0=take(g)[:],
                                         scalar=PT[:, COL_B1 + c:COL_B1 + c + 1],
                                         in1=SIG[n % 2], op0=ALU.add, op1=ALU.mult).then_inc(free["D"], 1)
                if h == 0:
                    continue
                dve.wait_ge(free["D"], emptied(g))
                o, p = CV[:, c, :], GT[:, c, :]

                def tap(j):
                    return PT[:, COL_DW + KC * j + c:COL_DW + KC * j + c + 1]
                link(dve.tensor_scalar(o, p, tap(CTAPS - 1), PT[:, COL_DWB + c:COL_DWB + c + 1],
                                       ALU.mult, ALU.add))
                for d in range(PTAPS[c] + 1, CTAPS):
                    link(dve.scalar_tensor_tensor(out=o[:, d:T], in0=p[:, 0:T - d],
                                                  scalar=tap(CTAPS - 1 - d), in1=o[:, d:T],
                                                  op0=ALU.mult, op1=ALU.add))
                dve.wait_ge(cv_ps, c + 1)
                tt(o[:, 1:HT], o[:, 1:HT], X0[:, 1:HT], ALU.add)
                tt(o[:, HT:T], o[:, HT:T], X1[:], ALU.add).then_inc(conv_ok, 1)
            dve.wait_ge(conv_ok, KC)
            dve.wait_ge(mu_ps, 1)
            for h in range(NH):
                s = slice(HT * h, HT * h + HT)
                link(dve.tensor_scalar(MUB[h], TB_[h][:], 1.0 / D, None, ALU.mult))
                for k in range(KC):
                    tt(CV[:, k, s], CV[:, k, s], MUB[h], ALU.subtract).then_inc(cen_ok, 1)
            for h in range(NH):
                s = slice(HT * h, HT * h + HT)
                dve.wait_ge(free["A"], emptied(GROUPS["var"] + h))
                link(dve.reciprocal(RSB[h], RSB[h]))
                dve.wait_ge(cen_ok, KC * h + KC)
                for k in range(KC):
                    tt(CV[:, k, s], CV[:, k, s], RSB[h], ALU.mult).then_inc(nrm_ok, 1)
            dve.wait_ge(gb_in[2], 32)
            project_in(GROUPS["w2"], 3, 1, GB1, TMP1, B2B)
            route(1)
            experts(1)
            for b in range(NB):
                if b == 5:
                    rms_apply(4, 0)
                combine(1, b)
            rms_apply(4, 1)


INPUTS = ["x", "c", "ada_w", "ada_b", "norm_mix_g", "norm_ffn_g", "hyb_w_in", "sgu_ln_g", "sgu_ln_b",
          "sgu_w", "sgu_b", "sconv_w", "hyb_w_out", "conf_w1", "conf_b1", "conf_dw_w", "conf_dw_b",
          "conf_ln_g", "conf_ln_b", "conf_w2", "conf_b2", "router_w", "router_bias", "moe_w_gate",
          "moe_w_up", "moe_w_down", "final_norm_g"]


def kernel(**inputs):
    import concourse.bacc as bacc
    from concourse.bass_utils import run_bass_kernel_spmd

    nc = bacc.Bacc("TRN2", target_bir_lowering=False, num_devices=1)
    arrays, aps = {}, {}
    for name in INPUTS:
        a = np.ascontiguousarray(inputs[name])
        arrays[f"in_{name}"] = a
        aps[name] = nc.dram_tensor(f"in_{name}", a.shape, mybir.dt.from_np(a.dtype),
                                   kind="ExternalInput").ap()
    out = nc.dram_tensor("out", (1, T, D), F32, kind="ExternalOutput").ap()
    trunk(nc, aps, out)
    r = run_bass_kernel_spmd(nc, [arrays], core_ids=[0])
    return r.results[0]["out"]
```
